# Optimizing a Trainium2 kernel written in Bass

```python
import jax, jax.numpy as jnp
from jax import lax
import numpy as np
import math

D_MODEL = 1024
BATCH = 1
SEQ = 256
DEPTH = 1

PLE_DIM = 256
CONV_WIDTH = D_MODEL // 2
CONV_HEADS = 8
CONV_K = 3
SGU_WIDTH = D_MODEL // 2
SGU_HEADS = 8
SGU_HEAD_DIM = SGU_WIDTH // SGU_HEADS
CHUNK = 128
MIX_WIDTH = CONV_WIDTH + SGU_WIDTH
IN_PROJ_WIDTH = 3 * CONV_WIDTH + 2 * SGU_WIDTH
N_GROUPS = 4
EXPERTS_PER_GROUP = 8
TOP_K_INNER = 2
D_EXPERT = D_MODEL // 2
EPS = 1e-6


def rmsnorm(x, g):
    xf = x.astype(jnp.float32)
    y = xf * lax.rsqrt(jnp.mean(xf * xf, axis=-1, keepdims=True) + EPS)
    return (y * g.astype(jnp.float32)).astype(x.dtype)

def layernorm(x, g):
    xf = x.astype(jnp.float32)
    mu = jnp.mean(xf, axis=-1, keepdims=True)
    xc = xf - mu
    y = xc * lax.rsqrt(jnp.mean(xc * xc, axis=-1, keepdims=True) + EPS)
    return (y * g.astype(jnp.float32)).astype(x.dtype)

def short_conv_mixer(b_gate, c_gate, x_in, w_conv):
    seq = x_in.shape[1]
    z = c_gate * x_in
    zp = jnp.pad(z, ((0, 0), (CONV_K - 1, 0), (0, 0)))
    conv = sum(zp[:, k:k + seq, :] * w_conv[k] for k in range(CONV_K))
    return b_gate * conv

def sgu_mixer(u, v, g_sgu, w_spatial, b_spatial):
    bsz, seq, _ = v.shape
    v = layernorm(v, g_sgu)
    vc = v.reshape(bsz, seq // CHUNK, CHUNK, SGU_HEADS, SGU_HEAD_DIM)
    causal = jnp.tril(jnp.ones((CHUNK, CHUNK), dtype=bool))
    ws = jnp.where(causal[None], w_spatial, jnp.zeros_like(w_spatial))
    mixed = jnp.einsum('hts,bcshd->bcthd', ws, vc) + b_spatial.T[None, None, :, :, None]
    return u * mixed.reshape(bsz, seq, SGU_WIDTH)

def hierarchical_moe(h, w_group, b_group, w_router, b_router, w_gate, w_up, w_down):
    bsz, seq, d = h.shape
    t = h.reshape(bsz * seq, d)
    g_logits = (t @ w_group).astype(jnp.float32) + b_group.astype(jnp.float32)
    g_prob = jax.nn.softmax(g_logits, axis=-1)
    g_w, g_idx = lax.top_k(g_prob, 1)
    e_logits = jnp.einsum('td,gde->tge', t, w_router).astype(jnp.float32) + b_router.astype(jnp.float32)
    e_sel = jnp.take_along_axis(e_logits, g_idx[:, :, None], axis=1)[:, 0]
    e_val, e_idx = lax.top_k(e_sel, TOP_K_INNER)
    e_w = jax.nn.softmax(e_val, axis=-1) * g_w
    inner = jnp.sum(jax.nn.one_hot(e_idx, EXPERTS_PER_GROUP, dtype=jnp.float32) * e_w[..., None], axis=1)
    comb = (jax.nn.one_hot(g_idx[:, 0], N_GROUPS, dtype=jnp.float32)[:, :, None]
            * inner[:, None, :]).astype(h.dtype)
    y = jnp.zeros_like(t)
    for g in range(N_GROUPS):
        a = jnp.einsum('td,edf->tef', t, w_gate[g])
        b = jnp.einsum('td,edf->tef', t, w_up[g])
        hid = jax.nn.silu(a) * b * comb[:, g, :, None]
        y = y + jnp.einsum('tef,efd->td', hid, w_down[g])
    return y.reshape(bsz, seq, d)

def first_inputs(seed: int = 0) -> dict:
    key = jax.random.key(seed)
    ks = jax.random.split(key, 24)
    f32 = jnp.float32
    n = lambda k, shape, scale: jax.random.normal(k, shape, f32) * scale
    gain = lambda k, shape: 1.0 + 0.05 * jax.random.normal(k, shape, f32)
    L, G, E = DEPTH, N_GROUPS, EXPERTS_PER_GROUP
    return {
        "x": n(ks[0], (BATCH, SEQ, D_MODEL), 1.0),
        "p": n(ks[1], (DEPTH, BATCH, SEQ, PLE_DIM), 1.0),
        "g_mix": gain(ks[2], (L, D_MODEL)),
        "w_in": n(ks[3], (L, D_MODEL, IN_PROJ_WIDTH), D_MODEL ** -0.5),
        "w_conv": n(ks[4], (L, CONV_K, CONV_WIDTH), CONV_K ** -0.5),
        "g_sgu": gain(ks[5], (L, SGU_WIDTH)),
        "w_spatial": n(ks[6], (L, SGU_HEADS, CHUNK, CHUNK), CHUNK ** -0.5),
        "b_spatial": 1.0 + n(ks[7], (L, SGU_HEADS, CHUNK), 0.1),
        "w_out": n(ks[8], (L, MIX_WIDTH, D_MODEL), MIX_WIDTH ** -0.5),
        "g_ffn": gain(ks[9], (L, D_MODEL)),
        "w_group": n(ks[10], (L, D_MODEL, G), D_MODEL ** -0.5),
        "b_group": n(ks[11], (L, G), 0.01),
        "w_router": n(ks[12], (L, G, D_MODEL, E), D_MODEL ** -0.5),
        "b_router": n(ks[13], (L, G, E), 0.01),
        "w_gate": n(ks[14], (L, G, E, D_MODEL, D_EXPERT), D_MODEL ** -0.5),
        "w_up": n(ks[15], (L, G, E, D_MODEL, D_EXPERT), D_MODEL ** -0.5),
        "w_down": n(ks[16], (L, G, E, D_EXPERT, D_MODEL), D_EXPERT ** -0.5),
        "g_ple": gain(ks[17], (L, D_MODEL)),
        "w_ple_gate": n(ks[18], (L, D_MODEL, D_MODEL), D_MODEL ** -0.5),
        "w_ple_proj": n(ks[19], (L, PLE_DIM, D_MODEL), PLE_DIM ** -0.5),
        "g_final": gain(ks[20], (D_MODEL,)),
    }

def first_block(x, p, g_mix, w_in, w_conv, g_sgu, w_spatial, b_spatial, w_out, g_ffn,
              w_group, b_group, w_router, b_router, w_gate, w_up, w_down,
              g_ple, w_ple_gate, w_ple_proj, g_final):
    splits = [CONV_WIDTH, 2 * CONV_WIDTH, 3 * CONV_WIDTH, 3 * CONV_WIDTH + SGU_WIDTH]
    for i in range(DEPTH):
        h = rmsnorm(x, g_mix[i])
        z = h @ w_in[i]
        b_gate, c_gate, x_in, u, v = jnp.split(z, splits, axis=-1)
        y_conv = short_conv_mixer(b_gate, c_gate, x_in, w_conv[i])
        y_sgu = sgu_mixer(jax.nn.gelu(u), jax.nn.gelu(v), g_sgu[i],
                          w_spatial[i], b_spatial[i])
        x = x + jnp.concatenate([y_conv, y_sgu], axis=-1) @ w_out[i]
        x = x + hierarchical_moe(rmsnorm(x, g_ffn[i]), w_group[i], b_group[i], w_router[i],
                                 b_router[i], w_gate[i], w_up[i], w_down[i])
        gate = jax.nn.sigmoid(rmsnorm(x, g_ple[i]) @ w_ple_gate[i])
        x = x + gate * (p[i] @ w_ple_proj[i])
    return rmsnorm(x, g_final)


CHUNK_2 = 64
CONV_DIM = D_MODEL // 2
CONV_WIDTH_2 = 31
N_HEADS = 8
HEAD_DIM = 64
ATT_DIM = N_HEADS * HEAD_DIM
QBLOCK = 128
D_FF = ((8 * D_MODEL + 3 * 256 - 1) // (3 * 256)) * 256
IN_COLS = 2 * CONV_DIM + 3 * ATT_DIM + 2 * D_MODEL


def rmsnorm_2(x, g):
    xf = x.astype(jnp.float32)
    y = xf * lax.rsqrt(jnp.mean(xf * xf, axis=-1, keepdims=True) + EPS)
    return (y * g.astype(jnp.float32)).astype(x.dtype)

def layernorm_2(x, g, b):
    xf = x.astype(jnp.float32)
    mu = jnp.mean(xf, axis=-1, keepdims=True)
    var = jnp.mean(jnp.square(xf - mu), axis=-1, keepdims=True)
    y = (xf - mu) * lax.rsqrt(var + EPS)
    return (y * g.astype(jnp.float32) + b.astype(jnp.float32)).astype(x.dtype)

def causal_depthwise_conv(u, w, b):
    k, c = w.shape
    up = jnp.pad(u, ((0, 0), (k - 1, 0), (0, 0)))
    y = lax.conv_general_dilated(
        up, w[:, None, :].astype(u.dtype), window_strides=(1,), padding='VALID',
        dimension_numbers=('NWC', 'WIO', 'NWC'), feature_group_count=c)
    return y + b.astype(u.dtype)

def stick_breaking_attention(q, k, v):
    s_len = q.shape[1]
    scale = 1.0 / math.sqrt(q.shape[-1])
    outs = []
    for i in range(s_len // QBLOCK):
        q0 = i * QBLOCK
        q1 = q0 + QBLOCK
        qb = q[:, q0:q1].astype(jnp.float32)
        kb = k[:, :q1].astype(jnp.float32)
        vb = v[:, :q1].astype(jnp.float32)
        z = jnp.einsum('bqhd,bkhd->bhqk', qb, kb) * scale
        t_idx = q0 + jnp.arange(QBLOCK)[:, None]
        s_idx = jnp.arange(q1)[None, :]
        mask = s_idx < t_idx
        log_1m = jnp.where(mask, jax.nn.log_sigmoid(-z), 0.0)
        rev_excl = lax.cumsum(log_1m, axis=3, reverse=True) - log_1m
        a = jnp.where(mask, jnp.exp(jax.nn.log_sigmoid(z) + rev_excl), 0.0)
        outs.append(jnp.einsum('bhqk,bkhd->bqhd', a, vb))
    return jnp.concatenate(outs, axis=1).astype(q.dtype)

def second_inputs(seed: int = 0) -> dict:
    key = jax.random.key(seed)
    ks = jax.random.split(key, 20)
    f32 = jnp.float32

    def w(k, shape, fan_in):
        return jax.random.normal(k, shape, f32) * (fan_in ** -0.5)

    def gain(k, n):
        return 1.0 + 0.05 * jax.random.normal(k, (n,), f32)

    def bias(k, n):
        return 0.02 * jax.random.normal(k, (n,), f32)

    return {
        'x': jax.random.normal(ks[0], (BATCH, SEQ, D_MODEL), f32),
        'norm_mix_pre': gain(ks[1], D_MODEL),
        'w_in': w(ks[2], (D_MODEL, IN_COLS), D_MODEL),
        'conv_dw_w': w(ks[3], (CONV_WIDTH_2, CONV_DIM), CONV_WIDTH_2),
        'conv_dw_b': bias(ks[4], CONV_DIM),
        'conv_ln_g': gain(ks[5], CONV_DIM),
        'conv_ln_b': bias(ks[6], CONV_DIM),
        'w_conv_branch': w(ks[7], (CONV_DIM, D_MODEL), CONV_DIM),
        'b_conv_branch': bias(ks[8], D_MODEL),
        'w_att_branch': w(ks[9], (ATT_DIM, D_MODEL), ATT_DIM),
        'w_out': w(ks[10], (D_MODEL, D_MODEL), D_MODEL),
        'norm_mix_post': gain(ks[11], D_MODEL),
        'norm_ffn_pre': gain(ks[12], D_MODEL),
        'w_ffn_up': w(ks[13], (D_MODEL, 2 * D_FF), D_MODEL),
        'w_ffn_down': w(ks[14], (D_FF, D_MODEL), D_FF),
        'norm_ffn_post': gain(ks[15], D_MODEL),
    }

def second_block(x, norm_mix_pre, w_in, conv_dw_w, conv_dw_b, conv_ln_g, conv_ln_b,
              w_conv_branch, b_conv_branch, w_att_branch, w_out, norm_mix_post,
              norm_ffn_pre, w_ffn_up, w_ffn_down, norm_ffn_post):
    b, s, d = x.shape
    for _ in range(DEPTH):
        h = rmsnorm_2(x, norm_mix_pre)
        proj = jnp.einsum('bsd,de->bse', h, w_in)
        splits = np.cumsum([2 * CONV_DIM, ATT_DIM, ATT_DIM, ATT_DIM, D_MODEL]).tolist()
        conv_in, q, k, v, g_conv, g_att = jnp.split(proj, splits, axis=-1)

        u = jax.nn.glu(conv_in, axis=-1)
        u = causal_depthwise_conv(u, conv_dw_w, conv_dw_b)
        u = jax.nn.silu(layernorm_2(u, conv_ln_g, conv_ln_b))
        conv_out = jnp.einsum('bsc,cd->bsd', u, w_conv_branch) + b_conv_branch

        q = q.reshape(b, s, N_HEADS, HEAD_DIM)
        k = k.reshape(b, s, N_HEADS, HEAD_DIM)
        v = v.reshape(b, s, N_HEADS, HEAD_DIM)
        att = stick_breaking_attention(q, k, v).reshape(b, s, ATT_DIM)
        att_out = jnp.einsum('bsc,cd->bsd', att, w_att_branch)

        merged = jax.nn.sigmoid(g_conv) * conv_out + jax.nn.sigmoid(g_att) * att_out
        mix = jnp.einsum('bsd,de->bse', merged, w_out)
        x = x + rmsnorm_2(mix, norm_mix_post)

        h = rmsnorm_2(x, norm_ffn_pre)
        gu = jnp.einsum('bsd,df->bsf', h, w_ffn_up)
        gate, up = jnp.split(gu, 2, axis=-1)
        ff = jnp.einsum('bsf,fd->bsd', jax.nn.silu(gate) * up, w_ffn_down)
        x = x + rmsnorm_2(ff, norm_ffn_post)
    return x


def setup_inputs(seed=0):
    out = dict(first_inputs(seed))
    for name, value in second_inputs(seed + 1).items():
        if name != "x":
            out[name + "_2"] = value
    return out


def reference(
    x, p, g_mix, w_in, w_conv, g_sgu, w_spatial, b_spatial, w_out, g_ffn, w_group, b_group,
    w_router, b_router, w_gate, w_up, w_down, g_ple, w_ple_gate, w_ple_proj, g_final,
    norm_mix_pre_2, w_in_2, conv_dw_w_2, conv_dw_b_2, conv_ln_g_2, conv_ln_b_2, w_conv_branch_2,
    b_conv_branch_2, w_att_branch_2, w_out_2, norm_mix_post_2, norm_ffn_pre_2, w_ffn_up_2,
    w_ffn_down_2, norm_ffn_post_2,
):
    x = first_block(
        x, p, g_mix, w_in, w_conv, g_sgu, w_spatial, b_spatial, w_out, g_ffn, w_group, b_group,
        w_router, b_router, w_gate, w_up, w_down, g_ple, w_ple_gate, w_ple_proj, g_final,
    )
    return second_block(
        x, norm_mix_pre_2, w_in_2, conv_dw_w_2, conv_dw_b_2, conv_ln_g_2, conv_ln_b_2,
        w_conv_branch_2, b_conv_branch_2, w_att_branch_2, w_out_2, norm_mix_post_2,
        norm_ffn_pre_2, w_ffn_up_2, w_ffn_down_2, norm_ffn_post_2,
    )


_drawn_inputs = setup_inputs


def setup_inputs(seed=0):
    import zlib

    import numpy as np

    out = dict(_drawn_inputs(seed))
    spreads = {}
    factors = {'b_group': 2.791,
     'b_router': 3.754,
     'g_ple': 6.17,
     'conv_ln_b_2': 5.093,
     'b_conv_branch_2': 2.992}
    for name, (base, spread) in spreads.items():
        noise = np.random.default_rng([zlib.crc32(name.encode()), seed]).standard_normal(out[name].shape)
        drawn = base * np.exp(spread * noise) if base else spread * noise
        out[name] = __import__('jax').numpy.asarray(drawn.astype(out[name].dtype))
    for name, factor in factors.items():
        out[name] = (out[name] * factor).astype(out[name].dtype)
    return out
```

```python
from contextlib import ExitStack

import numpy as np

import concourse.bass as bass
from concourse import mybir

F32 = mybir.dt.float32
I32 = mybir.dt.int32
ALU = mybir.AluOpType
ACT = mybir.ActivationFunctionType
AX = mybir.AxisListType.X

T = 256
D = 1024
NE = 32
CAP = 42
NB = 11
EPS = 1e-6
RING = 8
SLOT = 4096

C_ID, C_U, C_TRI, C_NM, C_IOTA, C_IX = 0, 128, 256, 384, 768, 810
N_CST = 818
VEC = {}
_at = 0
for _n, _w in (("g_mix", 8), ("w_conv", 12), ("g_sgu", 4), ("g_ffn", 8), ("g_ple", 8), ("g_final", 8),
               ("pre2", 8), ("dw_w", 124), ("dw_b", 4), ("ln_g", 4), ("ln_b", 4), ("b_cb", 8), ("post2", 8),
               ("fpre2", 8)):
    VEC[_n] = _at
    _at += _w
N_VEC = _at

BATCHES = [list(range(3 * b, min(3 * b + 3, NE))) for b in range(NB)]


def moe_order():
    out = []
    for e in range(NE + 1):
        if e < NE:
            out += [("g", e), ("u", e)]
        if e >= 1:
            out.append(("d", e - 1))
    return out


def stream():
    out = [("in1", i) for i in range(5)] + [("out1", i) for i in range(2)] + [("pproj", 0)]
    out += moe_order()
    out += [("pgate", i) for i in range(2)] + [("in2", i) for i in range(9)]
    out += [("cb", 0), ("ab", 0)] + [("out2", i) for i in range(2)]
    out += [("fup", i) for i in range(11)] + [("fdn", i) for i in range(6)]
    return out


def build(nc, dr, out_ap):
    ctx = ExitStack()
    with ctx:
        def sem(name):
            return ctx.enter_context(nc.semaphore(name))

        ring = ctx.enter_context(nc.sbuf_tensor("ring", [128, RING, SLOT], F32))
        cst = ctx.enter_context(nc.sbuf_tensor("cst", [128, N_CST], F32))
        vec = ctx.enter_context(nc.sbuf_tensor("vec", [128, N_VEC], F32))
        wr = ctx.enter_context(nc.sbuf_tensor("wr", [128, 8, 36], F32))
        ones = ctx.enter_context(nc.sbuf_tensor("ones", [128, 3, 128], F32))
        flag = ctx.enter_context(nc.sbuf_tensor("flag", [128, 1], I32))
        eps = ctx.enter_context(nc.sbuf_tensor("eps", [128, 1], F32))
        NAR = 18700
        arena = ctx.enter_context(nc.sbuf_tensor("arena", [128, NAR], F32))
        ps = [ctx.enter_context(nc.psum_tensor(f"ps{i}", [128, 512], F32)) for i in range(8)]

        def A(at, *shape):
            n = 1
            for s in shape:
                n *= s
            assert at + n <= NAR, (at, n)
            v = arena[:, at:at + n]
            if len(shape) == 2:
                v = v.rearrange("p (a b) -> p a b", a=shape[0])
            elif len(shape) == 3:
                v = v.rearrange("p (a b c) -> p a b c", a=shape[0], b=shape[1])
            return v

        names = ("pe", "dve", "act", "pool", "sp")
        queue = {n: [] for n in names}
        done_sem = {n: sem("done_" + n) for n in names}
        count = {n: 0 for n in names}
        seen = {n: {} for n in names}

        def wait(eng, toks):
            for tok in toks:
                s, v = tok
                if seen[eng].get(id(s), 0) < v:
                    seen[eng][id(s)] = v
                    queue[eng].append(lambda e, s=s, v=v: e.wait_ge(s, v))

        def op(eng, fn, *toks):
            wait(eng, toks)
            count[eng] += 1
            s = done_sem[eng]
            queue[eng].append(lambda e: fn(e).then_inc(s, 1))
            return (s, count[eng])

        def last(eng):
            return (done_sem[eng], count[eng])

        def all_last():
            return [last(n) for n in ("pe", "dve", "act") if count[n]]

        def load(eng, dst, src, s, *toks):
            wait(eng, toks)
            queue[eng].append(lambda e: e.dma_start(dst, src).then_inc(s, 16))
            return (s, 16)

        def mms(lst, *toks):
            wait("pe", toks)
            for o, l, r, a, z in lst[:-1]:
                queue["pe"].append(lambda e, o=o, l=l, r=r, a=a, z=z: e.matmul(
                    o, l, r, start=a, stop=z, skip_group_check=True))
            o, l, r, a, z = lst[-1]
            return op("pe", lambda e: e.matmul(o, l, r, start=a, stop=z, skip_group_check=True))

        def tts(lst, ident, *toks):
            wait("pe", toks)
            for o, i in lst[:-1]:
                queue["pe"].append(lambda e, o=o, i=i: e.transpose(o, i, ident))
            o, i = lst[-1]
            return op("pe", lambda e: e.transpose(o, i, ident))

        bank_free = [[] for _ in range(8)]

        def tt(o, a, b, f, *toks, eng="dve"):
            return op(eng, lambda e: e.tensor_tensor(o, a, b, f), *toks)

        def ts(o, a, s1, s2, f0, f1, *toks, eng="dve"):
            if f1 is None:
                return op(eng, lambda e: e.tensor_scalar(o, a, s1, s2, f0), *toks)
            return op(eng, lambda e: e.tensor_scalar(o, a, s1, s2, f0, f1), *toks)

        def stt(o, a, s, b, f0, f1, *toks):
            return op("dve", lambda e: e.scalar_tensor_tensor(out=o, in0=a, scalar=s, in1=b, op0=f0, op1=f1), *toks)

        def act(o, a, f, *toks, **kw):
            return op("act", lambda e: e.activation(o, a, f, **kw), *toks)

        def red(o, a, f, *toks):
            return op("dve", lambda e: e.tensor_reduce(o, a, AX, f), *toks)

        M, ADD, SUB, MAX = ALU.mult, ALU.add, ALU.subtract, ALU.max

        order = stream()
        index = {k: i for i, k in enumerate(order)}
        ring_sem = [sem(f"ring{i}") for i in range(RING)]
        freed = {}

        def slot(key):
            i = index[key]
            return ring[:, i % RING, :], (ring_sem[i % RING], 16 * (i // RING + 1))

        def free(key, tok):
            freed[index[key]] = tok

        ident = cst[:, C_ID:C_ID + 128]
        U = cst[:, C_U:C_U + 128]
        tri = cst[:, C_TRI:C_TRI + 128]
        nm = cst[:, C_NM:C_NM + 384]
        iota = cst[:, C_IOTA:C_IOTA + CAP]
        ix8 = cst[:, C_IX:C_IX + 8]
        one, inv1024, inv512 = ones[:, 0, :], ones[:, 1, :], ones[:, 2, :]

        def vcol(name, i):
            return vec[:, VEC[name] + i:VEC[name] + i + 1]

        XT = A(0, 8, 256)
        XK = A(2048, 2, 1024)
        H1 = A(4096, 8, 256)
        MIX = A(6144, 8, 256)
        PP = A(8192, 8, 256)
        SQ = A(10240, 8, 256)
        o = 12288
        VG = A(o, 2, 512)
        UG = A(o + 1024, 4, 256)
        Z = A(o + 2048, 4, 258)
        CR = A(o + 3080, 4, 256)
        PT = A(o + 4104, 2, 256)
        R1B = A(o + 4616, 256)
        BB = A(o + 4872, 4, 128)
        SM = A(o + 5384, 720)
        WS = PP

        t_xT = load("act", XT, dr["xT"], sem("l_xT"))
        t_vec = load("act", vec[:], dr["vec"], sem("l_vec"))
        t_xk = load("act", XK, dr["x"], sem("l_xk"))
        t_cst = load("act", cst[:], dr["cst"], sem("l_cst"))
        t_wr = load("act", wr[:], dr["wr"], sem("l_wr"))
        t_ws = load("act", WS[:, 0:4, :].rearrange("p a b -> p (a b)"), dr["wsT"], sem("l_ws"))
        s_bb = sem("l_bb")
        load("act", BB[0:64], dr["b_sp"][0:1, :, :].partition_broadcast(64), s_bb)
        load("act", BB[64:128], dr["b_sp"][1:2, :, :].partition_broadcast(64), s_bb)
        t_bb = (s_bb, 32)
        t_pT = load("act", PT, dr["pT"], sem("l_pT"))
        LB = SM[:, 0:36]
        t_lb = load("act", LB, dr["lbias"].partition_broadcast(128), sem("l_lb"))

        t_eps = op("dve", lambda e: e.memset(eps[:], EPS))
        op("dve", lambda e: e.memset(ones[:, 0, :], 1.0))
        op("dve", lambda e: e.memset(ones[:, 1, :], 1.0 / 1024))
        t_ones = op("dve", lambda e: e.memset(ones[:, 2, :], 1.0 / 512))
        t_zpad = op("dve", lambda e: e.memset(Z[:, :, 0:2], 0.0))

        def scale_cols(dst, src, name, *toks):
            return [ts(dst[:, c, :], src[:, c, :], vcol(name, c), None, M, None, *toks) for c in range(8)]

        def squares(dst, src, toks):
            return [act(dst[:, c, :], src[:, c, :], ACT.Square, toks[c]) for c in range(len(toks))]

        def mean_pe(bank, at, src, w, toks):
            n = len(toks)
            wait("pe", bank_free[bank])
            for c in range(n):
                tok = mms([(ps[bank][:, at:at + 256], w, src[:, c, :], c == 0, c == n - 1)], toks[c])
            return tok

        def rsqrt(dst, src, *toks):
            a = act(dst, src, ACT.Sqrt, t_eps, *toks, bias=eps[:, 0:1])
            return op("dve", lambda e: e.reciprocal(dst, dst), a)

        XG = SQ
        t_xg = scale_cols(XG, XT, "g_mix", t_xT, t_vec)
        SQ0 = MIX
        t_sq = squares(SQ0, XT, [t_xT] * 8)
        RT = SM[:, 40:42]
        for i in range(2):
            t_rt = act(VG.rearrange("p a b -> p (a b)"), XK[:, i, :], ACT.Square, t_xk, last("act"), scale=1.0 / 32,
                       accum_out=RT[:, i:i + 1])
        t_rt = rsqrt(RT, RT, t_rt)

        w, t_w = slot(("in1", 0))
        w = w.rearrange("p (c n) -> p c n", c=8)
        t_v = []
        for i in range(2):
            for c in range(8):
                tok = mms([(ps[i][:, :], XG[:, c, i * 128:i * 128 + 128], w[:, c, :], c == 0, c == 7)], t_w, t_xg[c])
            t_v.append(tok)
            if i == 0:
                wait("pe", [t_ones])
                t_m = mean_pe(2, 0, SQ0, inv1024, t_sq)
        free(("in1", 0), t_v[1])
        t_r1b = rsqrt(R1B, ps[2][:, 0:256], t_m)
        bank_free[2] = [t_r1b]
        t_h1 = [tt(H1[:, c, :], XG[:, c, :], R1B, M, t_r1b, t_xg[c]) for c in range(8)]
        VS = SM[:, 42:44]
        VM = SM[:, 44:46]
        t_g = []
        for i in range(2):
            t_g.append(act(VG[:, i, :], ps[i][:, :], ACT.Gelu_apprx_tanh, t_v[i], t_rt, scale=RT[:, i:i + 1],
                           accum_out=VS[:, i:i + 1]))
            bank_free[i] = [t_g[i]]
        t = ts(VM, VS, -1.0 / 512, None, M, None, t_g[1])
        t_xc = [ts(VG[:, i, :], VG[:, i, :], VM[:, i:i + 1], None, ADD, None, t, t_g[i]) for i in range(2)]
        VV = SM[:, 46:48]
        for i in range(2):
            t = act(SM[:, 200:712], VG[:, i, :], ACT.Square, t_xc[i], last("act"), accum_out=VV[:, i:i + 1])
        t = ts(VV, VV, 1.0 / 512, None, M, None, t)
        t = rsqrt(VV, VV, t)
        t_vn = [ts(VG[:, i, :], VG[:, i, :], VV[:, i:i + 1], None, M, None, t) for i in range(2)]

        def project(key, n_out, src, t_src, evac, banks, c_n=8, at=0):
            w, t_w = slot(key)
            w = w.rearrange("p (c n) -> p c n", c=c_n)
            for j in range(n_out):
                b = banks[j % len(banks)]
                wait("pe", bank_free[b])
                for c in range(c_n):
                    tok = mms([(ps[b][:, 0:256], w[:, c, at + j * 128:at + j * 128 + 128], src[:, c, :],
                                c == 0, c == c_n - 1)], t_w, t_src[c])
                bank_free[b] = evac(j, ps[b][:, 0:256], tok)
            return tok

        t_u = []

        def ev_u(j, p, tok):
            t_u.append(act(UG[:, j, :], p, ACT.Gelu_apprx_tanh, tok))
            return [t_u[-1]]

        free(("in1", 1), project(("in1", 1), 4, H1, t_h1, ev_u, [3, 4, 5, 6]))
        t_c = []

        def ev_c(j, p, tok):
            t_c.append(act(CR[:, j, :], p, ACT.Copy, tok))
            return [t_c[-1]]

        free(("in1", 2), project(("in1", 2), 4, H1, t_h1, ev_c, [0, 1, 2, 7]))
        t_cv = []

        def ev_x(j, p, tok):
            z = Z[:, j, 2:258]
            a = tt(z, p, CR[:, j, :], M, tok, t_c[j], t_zpad)
            k = ts(CR[:, j, :], z, vcol("w_conv", 8 + j), None, M, None, a)
            k = stt(CR[:, j, :], Z[:, j, 1:257], vcol("w_conv", 4 + j), CR[:, j, :], M, ADD, k)
            t_cv.append(stt(CR[:, j, :], Z[:, j, 0:256], vcol("w_conv", j), CR[:, j, :], M, ADD, k))
            return [a]

        free(("in1", 3), project(("in1", 3), 4, H1, t_h1, ev_x, [3, 4, 5, 6]))
        t_mix = []

        def ev_b(j, p, tok):
            t_mix.append(tt(MIX[:, j, :], p, CR[:, j, :], M, tok, t_cv[j], t_m))
            return [t_mix[-1]]

        free(("in1", 4), project(("in1", 4), 4, H1, t_h1, ev_b, [0, 1, 2, 7]))
        wsv = WS[:, 0:4, :].rearrange("p a (h t) -> p (a h) t", h=2)
        t_msk = op("pool", lambda e: e.affine_select(
            out=wsv, in_=wsv, compare_op=ALU.is_ge, fill=0.0, base=0, pattern=[[0, 8], [1, 128]],
            channel_multiplier=-1), t_ws)
        t_s = []
        for j in range(4):
            b = 3 + j
            wait("pe", bank_free[b] + [t_msk] + t_vn)
            lst = []
            for hh in range(2):
                h = 2 * j + hh
                for i in range(2):
                    lst.append((ps[b][64 * hh:64 * hh + 64, i * 128:i * 128 + 128], VG[:, i, h * 64:h * 64 + 64],
                                wsv[:, h, :], i == 0, True))
            tok = mms(lst)
            mx = MIX[:, 4 + j, :].rearrange("p (i t) -> p i t", i=2)
            k = None
            for i in range(2):
                k = stt(mx[:, i, :], ps[b][:, i * 128:i * 128 + 128], vcol("g_sgu", j), BB[:, j, :], M, ADD, tok, t_bb,
                        t_m)
            bank_free[b] = [k]
            t_mix.append(tt(MIX[:, 4 + j, :], MIX[:, 4 + j, :], UG[:, j, :], M, k, t_u[j]))
        t_x1 = {}
        for n in range(2):
            w, t_w = slot(("out1", n))
            w = w.rearrange("p (c n) -> p c n", c=8)
            for i in range(2):
                b = [0, 1, 2, 7][2 * n + i]
                wait("pe", bank_free[b])
                for c in range(8):
                    tok = mms([(ps[b][:, :], MIX[:, c, i * 128:i * 128 + 128], w[:, c, :], c == 0, c == 7)],
                              t_w, t_mix[c])
                x = XK[:, i, n * 512:n * 512 + 512]
                t_x1[i, n] = tt(x, x, ps[b][:, :], ADD, tok, t_xk)
                bank_free[b] = [t_x1[i, n]]
            free(("out1", n), tok)
        t_x1a = t_x1[1, 1]
        R2 = SM[:, 48:50]
        for i in range(2):
            t = act(SQ[:, 0:4, :].rearrange("p a b -> p (a b)"), XK[:, i, :], ACT.Square, t_x1a, last("act"), last("pe"),
                    scale=1.0 / 32, accum_out=R2[:, i:i + 1])
        t_r2 = rsqrt(R2, R2, t)
        t_wrg = None
        for c in range(8):
            t_wrg = ts(wr[:, c, :], wr[:, c, :], vcol("g_ffn", c), None, M, None, t_wr)
        t_xT1 = []
        for q in range(4):
            b = 3 + q
            tok = tts([(ps[b][:, (cc * 2 + i) * 128:(cc * 2 + i) * 128 + 128],
                        XK[:, i, (2 * q + cc) * 128:(2 * q + cc) * 128 + 128]) for cc in range(2) for i in range(2)],
                      ident, t_x1a, t_cst, *bank_free[b])
            dst = XT[:, 2 * q:2 * q + 2, :].rearrange("p a b -> p (a b)")
            if q % 2:
                k = act(dst, ps[b][:, :], ACT.Copy, tok)
            else:
                k = op("dve", lambda e, dst=dst, b=b: e.tensor_copy(dst, ps[b][:, :]), tok)
            bank_free[b] = [k]
            t_xT1 += [k, k]
        wait("pe", [t_wrg] + bank_free[0] + bank_free[1])
        for i in range(2):
            for c in range(8):
                tok = mms([(ps[i][:, 0:36], XT[:, c, i * 128:i * 128 + 128], wr[:, c, :], c == 0, c == 7)], t_xT1[c])
        t_lg = tok
        X1H = H1
        t_x1h = [act(X1H[:, :, :].rearrange("p a b -> p (a b)")[:, i * 1024:i * 1024 + 1024], XK[:, i, :], ACT.Copy,
                     t_r2, scale=R2[:, i:i + 1]) for i in range(2)]
        x1h = A(4096, 2, 1024)
        t_pp = []
        w, t_w = slot(("pproj", 0))
        w = w.rearrange("p (c n) -> p c n", c=4)
        for j in range(8):
            b = [2, 7, 3, 4][j % 4]
            tok = mms([(ps[b][:, 0:256], w[:, c, j * 128:j * 128 + 128], PT[:, c, :], c == 0, c == 1)
                       for c in range(2)], t_w, t_pT, *bank_free[b])
            k = act(PP[:, j, :], ps[b][:, 0:256], ACT.Copy, tok, last("pe"))
            bank_free[b] = [k]
            t_pp.append(k)
        free(("pproj", 0), tok)

        q = [50]

        def small(n):
            v = SM[:, q[0]:q[0] + n]
            q[0] += n
            assert q[0] <= 720
            return v

        LG = small(72).rearrange("p (i n) -> p i n", i=2)
        for i in range(2):
            t = stt(LG[:, i, :], ps[i][:, 0:36], R2[:, i:i + 1], LB, M, ADD, t_lg, t_r2, t_lb)
            bank_free[i] = [t]
        GL = LG[:, :, 0:4]
        EL = LG[:, :, 4:36].rearrange("p i (g e) -> p i g e", g=4)

        def first_max(src, n, t):
            mx = small(2)
            eq = small(2 * n).rearrange("p (i n) -> p i n", i=2)
            mn = small(2)
            t = red(mx, src, ALU.max, t)
            tm = t
            t = tt(eq, src, mx.unsqueeze(2).to_broadcast([128, 2, n]), ALU.is_equal, t)
            t = tt(eq, eq, ix8[:, 0:n].unsqueeze(1).to_broadcast([128, 2, n]), M, t, t_cst)
            t = red(mn, eq, ALU.min, t)
            t = tt(eq, ix8[:, 0:n].unsqueeze(1).to_broadcast([128, 2, n]), mn.unsqueeze(2).to_broadcast([128, 2, n]),
                   ALU.is_equal, t)
            return mx, eq, tm, t

        gm, goh, tm, t_goh = first_max(GL, 4, t)
        ngm = small(2)
        t = ts(ngm, gm, -1.0, None, M, None, tm)
        gex = small(8).rearrange("p (i n) -> p i n", i=2)
        gs = small(2)
        for i in range(2):
            t_gs = act(gex[:, i, :], GL[:, i, :], ACT.Exp, t, bias=ngm[:, i:i + 1], accum_out=gs[:, i:i + 1])
        em = small(64).rearrange("p (i g e) -> p i g e", i=2, g=4)
        t = None
        for i in range(2):
            t = tt(em[:, i], EL[:, i], goh[:, i, :].unsqueeze(2).to_broadcast([128, 4, 8]), M, t_goh)
        es = small(16).rearrange("p (i e) -> p i e", i=2)
        for i in range(2):
            tr = red(es[:, i, :], em[:, i].rearrange("p g e -> p e g"), ALU.add, t)
        v1, oh1, _, t1 = first_max(es, 8, tr)
        e2 = small(16).rearrange("p (i e) -> p i e", i=2)
        t = stt(e2, oh1, -1e30, es, M, ADD, t1)
        v2, oh2, _, t2 = first_max(e2, 8, t)
        dv = small(2)
        t = tt(dv, v2, v1, SUB, t2)
        ex = small(2)
        t_ex = act(ex, dv, ACT.Exp, t)
        den = small(2)
        t = ts(den, ex, 1.0, None, ADD, None, t_ex)
        t = tt(den, den, gs, M, t, t_gs)
        w1 = small(2)
        t = op("dve", lambda e: e.reciprocal(w1, den), t)
        w2 = small(2)
        t = tt(w2, w1, ex, M, t)
        inn = small(16).rearrange("p (i e) -> p i e", i=2)
        inb = small(16).rearrange("p (i e) -> p i e", i=2)
        for i in range(2):
            k = ts(inn[:, i, :], oh1[:, i, :], w1[:, i:i + 1], None, M, None, t)
        for i in range(2):
            t = stt(inn[:, i, :], oh2[:, i, :], w2[:, i:i + 1], inn[:, i, :], M, ADD, k)
        k = tt(inb, oh1, oh2, ADD, t2)
        comb = small(64).rearrange("p (i g e) -> p i g e", i=2, g=4)
        mask = small(64).rearrange("p (i g e) -> p i g e", i=2, g=4)
        for i in range(2):
            gb = goh[:, i, :].unsqueeze(2).to_broadcast([128, 4, 8])
            t_mk = tt(mask[:, i], inb[:, i, :].unsqueeze(1).to_broadcast([128, 4, 8]), gb, M, k)
            t_cb = tt(comb[:, i], inn[:, i, :].unsqueeze(1).to_broadcast([128, 4, 8]), gb, M, t)
        mk = mask.rearrange("p i g e -> p i (g e)")
        cb = comb.rearrange("p i g e -> p i (g e)")
        wait("pe", bank_free[0] + bank_free[1] + [t_mk])
        t_pos = mms([(ps[0][:, 0:32], U, mk[:, 0, :], True, True),
                     (ps[0][:, 32:64], U, mk[:, 1, :], True, False),
                     (ps[0][:, 32:64], one, mk[:, 0, :], False, True),
                     (ps[0][:, 64:96], one, mk[:, 0, :], True, False),
                     (ps[0][:, 64:96], one, mk[:, 1, :], False, True)])
        pos = small(64).rearrange("p (i e) -> p i e", i=2)
        t = stt(pos, ps[0][:, 0:64].rearrange("p (i e) -> p i e", i=2), 1.0, mk, ADD, M, t_pos)
        t_ps = ts(pos, pos, -1.0, None, ADD, None, t)
        cm = small(1)
        t = red(cm, ps[0][:, 64:96], ALU.max, t_pos)
        bank_free[0] = [t]
        t_flag = ts(flag[:], cm, float(CAP), None, ALU.is_gt, None, t)

        o = 12288
        YC = A(2048, 1024)
        SB = [A(o + 252 * k, 2, 3, CAP) for k in range(2)]
        SC = A(o + 504, 2, 3, CAP)
        SCT = [A(o + 756 + 256 * k, 256) for k in range(2)]
        YT = A(o + 1268, 8, 3 * CAP)
        SG = [A(o + 2276 + 168 * k, 4, CAP) for k in range(2)]
        HD = [A(o + 2612 + 168 * k, 4, CAP) for k in range(2)]
        HC = [A(6144 + 1008 * k, 8, 3 * CAP) for k in range(2)]
        assert o + 2948 <= o + 4104
        fence = all_last()
        for n in ("dve", "act", "pe"):
            wait(n, fence)
        t_hc, t_sct, t_sb = {}, {}, {}
        gat_bank = [4, 5]
        t_ytr = [None]
        t_gat = {}
        t_scat = {}

        def gather(b):
            k = b % 2
            n = len(BATCHES[b])
            e0 = BATCHES[b][0]
            old = [t_gat[b - 2], t_scat[b - 2]] if b >= 2 else []
            for i in range(2):
                io = iota.unsqueeze(1).to_broadcast([128, n, CAP])
                pb = pos[:, i, e0:e0 + n].unsqueeze(2).to_broadcast([128, n, CAP])
                t = tt(SB[k][:, i, 0:n, :], io, pb, ALU.is_equal, t_ps, *old)
            w_old = [t_sct[b - 1]] if b else []
            for i in range(2):
                c2 = cb[:, i, e0:e0 + n].unsqueeze(2).to_broadcast([128, n, CAP])
                ts_ = tt(SC[:, i, 0:n, :], SB[k][:, i, 0:n, :], c2, M, t, t_cb, *w_old)
            m = n * CAP
            for q in range(2):
                bk = gat_bank[q]
                lst = []
                for c in range(4):
                    for i in range(2):
                        lst.append((ps[bk][:, c * m:c * m + m], x1h[:, i, (4 * q + c) * 128:(4 * q + c) * 128 + 128],
                                    SB[k][:, i, 0:n, :].rearrange("p e s -> p (e s)"), i == 0, i == 1))
                tok = mms(lst, t, *t_x1h, *bank_free[bk])
                g = vec[:, VEC["g_ffn"] + 4 * q:VEC["g_ffn"] + 4 * q + 4].unsqueeze(2).to_broadcast([128, 4, m])
                t_hc[b] = tt(HC[k][:, 4 * q:4 * q + 4, 0:m], ps[bk][:, 0:4 * m].rearrange("p (c s) -> p c s", c=4), g,
                             M, tok, *([t_last[b - 2]] if b >= 2 else []))
                bank_free[bk] = [t_hc[b]]
            t_gat[b] = tok
            bk = 6
            tok = tts([(ps[bk][0:m, i * 128:i * 128 + 128], SC[:, i, 0:n, :].rearrange("p e s -> p (e s)"))
                       for i in range(2)], ident, ts_, *bank_free[bk])
            t_sct[b] = act(SCT[k][0:m, :], ps[bk][0:m, 0:256], ACT.Copy, tok, *([t_scat[b - 2]] if b >= 2 else []))
            bank_free[bk] = [t_sct[b]]

        t_last = {}
        t_a, t_hid, t_y = {}, {}, {}

        def gate_up(e):
            b, r = e // 3, e % 3
            bk = e % 2
            hc = HC[b % 2]
            for z, key in enumerate(("g", "u")):
                w, t_w = slot((key, e))
                w = w.rearrange("p (c n) -> p c n", c=8)
                lst = []
                for j in range(4):
                    at = (4 * z + j) * CAP
                    for c in range(8):
                        lst.append((ps[bk][:, at:at + CAP], w[:, c, j * 128:j * 128 + 128],
                                    hc[:, c, r * CAP:r * CAP + CAP], c == 0, c == 7))
                tok = mms(lst, t_w, t_hc[b], *bank_free[bk])
                free((key, e), tok)
            t_last[b] = tok
            k = e % 2
            old = [t_y[e - 2]] if e >= 2 else []
            s = act(SG[k], ps[bk][:, 0:4 * CAP].rearrange("p (j s) -> p j s", j=4), ACT.Silu, tok,
                    *([t_hid[e - 2]] if e >= 2 else []))
            t_hid[e] = tt(HD[k], ps[bk][:, 4 * CAP:8 * CAP].rearrange("p (j s) -> p j s", j=4), SG[k], M, s, tok, *old)
            bank_free[bk] = [t_hid[e]]

        def down(e):
            r = e % 3
            bk = 2 + e % 2
            w, t_w = slot(("d", e))
            w = w.rearrange("p (f n) -> p f n", f=4)
            lst = []
            for j in range(8):
                for f in range(4):
                    lst.append((ps[bk][:, j * CAP:j * CAP + CAP], w[:, f, j * 128:j * 128 + 128], HD[e % 2][:, f, :],
                                f == 0, f == 3))
            tok = mms(lst, t_w, t_hid[e], *bank_free[bk])
            free(("d", e), tok)
            t_y[e] = tok
            wy = [t_ytr[0]] if t_ytr[0] else []
            k = act(YT[:, :, r * CAP:r * CAP + CAP], ps[bk][:, 0:8 * CAP].rearrange("p (j s) -> p j s", j=8), ACT.Copy,
                    tok, *wy)
            bank_free[bk] = [k]
            return k

        t_acc = {j: t_xT1[2 * j] for j in range(4)}

        def scatter(b, t_yt):
            m = len(BATCHES[b]) * CAP
            k = b % 2
            tyc = []
            for q in range(2):
                bk = 6 + q
                tok = tts([(ps[bk][0:m, c * 128:c * 128 + 128], YT[:, 4 * q + c, 0:m]) for c in range(4)], ident, t_yt,
                          *bank_free[bk])
                old = [t_scat[b - 1]] if b else []
                kk = op("dve", lambda e, q=q, bk=bk: e.tensor_copy(YC[0:m, q * 512:q * 512 + 512], ps[bk][0:m, :]), tok,
                        *old)
                bank_free[bk] = [kk]
                tyc.append(kk)
            t_ytr[0] = tok
            for q in range(4):
                bk = [4, 5, 6, 7][q]
                tok = mms([(ps[bk][:, z * 256:z * 256 + 256], YC[0:m, (2 * q + z) * 128:(2 * q + z) * 128 + 128],
                            SCT[k][0:m, :], True, True) for z in range(2)], tyc[q // 2], t_sct[b], *bank_free[bk])
                x = XT[:, 2 * q:2 * q + 2, :].rearrange("p a b -> p (a b)")
                t_acc[q] = tt(x, x, ps[bk][:, :], ADD, tok, t_acc[q])
                bank_free[bk] = [t_acc[q]]
            t_scat[b] = tok

        gather(0)
        for e in range(NE + 1):
            if e < NE:
                gate_up(e)
            if e >= 1:
                t_yt = down(e - 1)
                if (e - 1) % 3 == 0 and e // 3 + 1 < NB:
                    gather((e - 1) // 3 + 1)
                if e - 1 == BATCHES[(e - 1) // 3][-1]:
                    scatter((e - 1) // 3, t_yt)

        fence = all_last()
        HO = A(10240, 8, 256)
        WG = [A(2048 + 1024 * k, 8, 128) for k in range(2)]
        OH = A(6144, 4, 256)
        WD = A(6144 + 1024, 4, 128)
        OS = A(6144 + 1536, 256)
        CO = A(o, 2, 32)
        COT = A(o + 64, 256)
        s_over = {n: sem("over_" + n) for n in ("pe", "dve", "act", "dma")}
        over = {n: [] for n in names}
        ocnt = {n: 0 for n in s_over}

        def oop(eng, fn, *toks):
            for s, v in toks:
                over[eng].append(lambda e, s=s, v=v: e.wait_ge(s, v))
            ocnt[eng] += 1
            over[eng].append(lambda e: fn(e).then_inc(s_over[eng], 1))
            return (s_over[eng], ocnt[eng])

        def oload(dst, src, *toks):
            for s, v in toks:
                over["pool"].append(lambda e, s=s, v=v: e.wait_ge(s, v))
            ocnt["dma"] += 16
            over["pool"].append(lambda e: e.dma_start(dst, src).then_inc(s_over["dma"], 16))
            return (s_over["dma"], ocnt["dma"])

        def omm(lst, *toks):
            for s, v in toks:
                over["pe"].append(lambda e, s=s, v=v: e.wait_ge(s, v))
            for o_, l, r, a, z in lst[:-1]:
                over["pe"].append(lambda e, o_=o_, l=l, r=r, a=a, z=z: e.matmul(
                    o_, l, r, start=a, stop=z, skip_group_check=True))
            o_, l, r, a, z = lst[-1]
            return oop("pe", lambda e: e.matmul(o_, l, r, start=a, stop=z, skip_group_check=True))

        t = None
        for c in range(8):
            for i in range(2):
                tp = oop("pe", lambda e, c=c, i=i: e.transpose(
                    ps[0][:, i * 128:i * 128 + 128], x1h[:, i, c * 128:c * 128 + 128], ident), *([t] if t else []))
            t = oop("dve", lambda e, c=c: e.tensor_scalar(HO[:, c, :], ps[0][:, 0:256], vcol("g_ffn", c), None, M), tp)
        k = oop("dve", lambda e: e.tensor_scalar(CO, pos, float(CAP) - 0.5, None, ALU.is_ge))
        k = oop("dve", lambda e: e.tensor_tensor(CO, CO, cb, M), k)
        for i in range(2):
            tp = oop("pe", lambda e, i=i: e.transpose(ps[0][0:32, i * 128:i * 128 + 128], CO[:, i, :], ident), k, t)
        t_ready = oop("dve", lambda e: e.tensor_copy(COT[0:32, :], ps[0][0:32, 0:256]), tp)
        t_od = t_ready
        t_wfree = t_dfree = None
        for x in range(NE):
            tb = omm([(ps[1][:, 0:256], ident[0:32, x:x + 1].to_broadcast([32, 128]), COT[0:32, :], True, True)],
                     t_od, t_ready)
            for j in range(4):
                tl = None
                for z, key in enumerate(("g", "u")):
                    src = dr["moe"][index[(key, x)] - 8].rearrange("p (c n) -> p c n", c=8)[:, :, j * 128:j * 128 + 128]
                    tl = oload(WG[z], src, *([t_wfree] if t_wfree else []))
                for z in range(2):
                    tp = omm([(ps[2 + z][:, 0:256], WG[z][:, c, :], HO[:, c, :], c == 0, c == 7) for c in range(8)],
                             tl, t_od, tb)
                t_wfree = tp
                ta = oop("act", lambda e: e.activation(OS, ps[2][:, 0:256], ACT.Silu), tp, t_od)
                t_od = oop("dve", lambda e: e.tensor_tensor(OS, OS, ps[3][:, 0:256], M), ta)
                t_od = oop("dve", lambda e, j=j: e.tensor_tensor(OH[:, j, :], OS, ps[1][:, 0:256], M), t_od)
            t_hd = t_od
            for j in range(8):
                src = dr["moe"][index[("d", x)] - 8].rearrange("p (f n) -> p f n", f=4)[:, :, j * 128:j * 128 + 128]
                tl = oload(WD, src, *([t_dfree] if t_dfree else []))
                tp = omm([(ps[4][:, 0:256], WD[:, f, :], OH[:, f, :], f == 0, f == 3) for f in range(4)], tl, t_od)
                t_dfree = tp
                t_od = oop("dve", lambda e, j=j: e.tensor_tensor(XT[:, j, :], XT[:, j, :], ps[4][:, 0:256], ADD), tp)

        def guard(eng):
            wait(eng, fence + [t_flag])

            def emit(e, eng=eng):
                v = e.value_load(flag[0:1, 0:1], min_val=0, max_val=1)
                with e.If(v > 0):
                    for f in over[eng]:
                        f(e)
                    e.wait_ge(*t_od)
            queue[eng].append(emit)

        t_moe = [t_acc[q] for q in range(4)]
        for eng in ("pe", "dve", "act", "pool"):
            guard(eng)

        XG = A(4096, 8, 256)
        SQ = A(6144, 8, 256)
        RB = A(o + 512, 4, 256)
        XN = A(2048, 8, 256)
        TM = A(o + 1536, 4, 256)
        t_xg = scale_cols(XG, XT, "g_ple", *t_moe)
        t_sq = squares(SQ, XT, [t_moe[c // 2] for c in range(8)])
        w, t_w = slot(("pgate", 0))
        t_p = []
        t_xn, t_g3, t_sq1, t_sq2 = [], [], [], []
        XN2 = A(8192, 8, 256)
        banks = [0, 1, 2, 3, 4, 5, 6]
        def ple_out(j):
            b, tok = t_p[j]
            k = j % 4
            a = tt(TM[:, k, :], ps[b][:, 0:256], RB[:, 0, :], M, tok, t_r3, *([t_xn[j - 4]] if j >= 4 else []))
            bank_free[b] = [a]
            a = act(TM[:, k, :], TM[:, k, :], ACT.Sigmoid, a)
            a = tt(TM[:, k, :], TM[:, k, :], PP[:, j, :], M, a, t_pp[j])
            a = tt(XT[:, j, :], XT[:, j, :], TM[:, k, :], ADD, a)
            t_xn.append(a)
            g = ts(XN[:, j, :], XT[:, j, :], vcol("g_final", j), None, M, None, a)
            t_g3.append(g)
            t_sq1.append(act(SQ[:, j, :], XT[:, j, :], ACT.Square, a, t_m))
            t_sq2.append(act(XN2[:, j, :], XN[:, j, :], ACT.Square, g))

        for j in range(8):
            if j == 1:
                t_m = mean_pe(7, 0, SQ, inv1024, t_sq)
                t_r3 = rsqrt(RB[:, 0, :], ps[7][:, 0:256], t_m)
                bank_free[7] = [t_r3]
            w, t_w = slot(("pgate", j // 4))
            w = w.rearrange("p (c n) -> p c n", c=8)
            b = banks[j % 7]
            wait("pe", bank_free[b])
            for c in range(8):
                tok = mms([(ps[b][:, 0:256], w[:, c, (j % 4) * 128:(j % 4) * 128 + 128], XG[:, c, :], c == 0, c == 7)],
                          t_w, t_xg[c])
            if j % 4 == 3:
                free(("pgate", j // 4), tok)
            t_p.append((b, tok))
            if j >= 1:
                ple_out(j - 1)
        ple_out(7)

        t_m1 = mean_pe(7, 0, SQ, inv1024, t_sq1)
        t_r4 = rsqrt(RB[:, 1, :], ps[7][:, 0:256], t_m1)
        bank_free[7] = [t_r4]
        t_m2 = mean_pe(6, 0, XN2, inv1024, t_sq2)
        a = tt(RB[:, 2, :], RB[:, 1, :], RB[:, 1, :], M, t_r4)
        a = tt(RB[:, 2, :], RB[:, 2, :], ps[6][:, 0:256], M, a, t_m2)
        bank_free[6] = [a]
        a = rsqrt(RB[:, 2, :], RB[:, 2, :], a)
        t_r45 = tt(RB[:, 2, :], RB[:, 2, :], RB[:, 1, :], M, a)
        H5 = A(6144, 8, 256)
        t_h5 = [stt(H5[:, c, :], XN[:, c, :], vcol("pre2", c), RB[:, 2, :], M, M, t_r45, t_m1, t_g3[c]) for c in range(8)]
        t_x4 = [tt(XT[:, c, :], XN[:, c, :], RB[:, 1, :], M, t_r4) for c in range(8)]
        SGC = A(2048, 8, 256)
        SGA = A(4096, 8, 256)
        CU = A(10240, 4, 286)
        CA = A(8192, 4, 256)
        QT = A(8192 + 1024, 4, 256)
        KT = A(o + 2560, 4, 256)
        VT = A(o + 3584, 2, 512)
        ZM = A(11384, 2, 384)
        o2 = o + 4608
        AB = A(o2, 2, 384)
        AT = A(o2 + 768, 4, 256)
        assert 11384 + 768 <= o

        GS = KT
        t_gs = []

        def ev_gs(j, p, tok):
            t_gs.append(act(GS[:, j, :], p, ACT.Sigmoid, tok))
            return [t_gs[-1]]

        free(("in2", 0), project(("in2", 0), 4, H5, t_h5, ev_gs, [0, 1, 2, 3]))
        t_cpad = op("dve", lambda e: e.memset(CU[:, :, 0:30], 0.0))
        t_glu = []

        def ev_glu(j, p, tok):
            t_glu.append(tt(CU[:, j, 30:286], p, GS[:, j, :], M, tok, t_gs[j]))
            return [t_glu[-1]]

        free(("in2", 1), project(("in2", 1), 4, H5, t_h5, ev_glu, [4, 5, 6, 7]))
        taps = []
        t_tap = {}

        def tap(j, k):
            src = CU[:, j, k:k + 256]
            wv = vec[:, VEC["dw_w"] + 4 * k + j:VEC["dw_w"] + 4 * k + j + 1]
            if k == 0:
                t_tap[j] = ts(CA[:, j, :], src, wv, vcol("dw_b", j), M, ADD, t_glu[j], t_cpad, t_m2)
            else:
                t_tap[j] = stt(CA[:, j, :], src, wv, CA[:, j, :], M, ADD, t_tap[j])

        for k in range(31):
            for j in range(4):
                taps.append((j, k))

        def some_taps(n):
            for _ in range(min(n, len(taps))):
                tap(*taps.pop(0))

        t_q, t_k, t_vv = [], [], []

        def ev_q(j, p, tok):
            t_q.append(act(QT[:, j, :], p, ACT.Copy, tok, t_m2))
            return [t_q[-1]]

        def ev_k(j, p, tok):
            t_k.append(act(KT[:, j, :], p, ACT.Copy, tok, t_glu[3]))
            return [t_k[-1]]

        free(("in2", 2), project(("in2", 2), 4, H5, t_h5, ev_q, [0, 1, 2, 3]))
        some_taps(32)
        free(("in2", 3), project(("in2", 3), 4, H5, t_h5, ev_k, [4, 5, 6, 7]))
        w, t_w = slot(("in2", 4))
        w = w.rearrange("p (c n) -> p c n", c=8)
        for i in range(2):
            lst = [(ps[i][:, :], H5[:, c, i * 128:i * 128 + 128], w[:, c, :], c == 0, c == 7) for c in range(8)]
            tok = mms(lst, t_w, *bank_free[i])
            t_vv.append(act(VT[:, i, :], ps[i][:, :], ACT.Copy, tok))
            bank_free[i] = [t_vv[i]]
        free(("in2", 4), tok)
        some_taps(16)
        ATT = CU
        t_att, t_zm, t_av = {}, {}, {}
        t_c2 = {}

        def scores(h):
            b = 2 + h % 2
            r = 64 * (h % 2)
            j = h // 2
            tok = mms([(ps[b][:, 0:256], KT[r:r + 64, j, 0:128], QT[r:r + 64, j, :], True, True),
                       (ps[b][:, 256:384], KT[r:r + 64, j, 128:256], QT[r:r + 64, j, 128:256], True, True)],
                      t_q[j], t_k[j], *bank_free[b])
            k = h % 2
            old = [t_c2[h - 2]] if h >= 2 else []
            t_zm[h] = stt(ZM[:, k, :], ps[b][:, 0:384], 0.125, nm, M, ADD, tok, *old)
            bank_free[b] = [t_zm[h]]
            old = [t_av[h - 2]] if h >= 2 else []
            x = AB[:, k, :]
            a = act(x, ZM[:, k, :], ACT.Abs, t_zm[h], *old)
            a = act(x, x, ACT.Exp, a, scale=-1.0)
            a = act(x, x, ACT.Ln, a, bias=1.0)
            return stt(x, ZM[:, k, :], 0.0, x, MAX, ADD, a)

        def suffix(h, t_p):
            b = 4 + h % 2
            k = h % 2
            x = AB[:, k, :]
            tok = mms([(ps[b][:, 0:256], tri, x[:, 0:256], True, False),
                       (ps[b][:, 128:256], one, x[:, 256:384], False, True),
                       (ps[b][:, 256:384], tri, x[:, 256:384], True, True)], t_p, *bank_free[b])
            a = tt(x, ZM[:, k, :], ps[b][:, 0:384], SUB, tok)
            t_c2[h] = a
            bank_free[b] = [a]
            return act(x, x, ACT.Exp, a)

        t_attT = [None] * 4
        pair = {}

        def values(h, t_a):
            b = 6 + (h // 2) % 2
            r = 64 * (h % 2)
            x = AB[:, h % 2, :]
            tok = mms([(ps[b][r:r + 64, 0:256], VT[:, 0, h * 64:h * 64 + 64], x[:, 0:256], True, False),
                       (ps[b][r:r + 64, 128:256], VT[:, 1, h * 64:h * 64 + 64], x[:, 256:384], False, True)],
                      t_a, *t_vv, *(bank_free[b] if h % 2 == 0 else []))
            t_av[h] = tok
            if h % 2:
                j = h // 2
                t_attT[j] = act(AT[:, j, :], ps[b][:, 0:256], ACT.Copy, tok)
                bank_free[b] = [t_attT[j]]


        p, a_ = {}, {}
        G0 = [("in2", 5), ("in2", 6), ("in2", 7), ("in2", 8)]
        t_sg = {}

        def gates(n, half):
            key = G0[n]
            w, t_w = slot(key)
            w = w.rearrange("p (c n) -> p c n", c=8)
            dst = SGC if n < 2 else SGA
            for j in (2 * half, 2 * half + 1):
                b = j % 2
                tok = mms([(ps[b][:, 0:256], w[:, c, j * 128:j * 128 + 128], H5[:, c, :], c == 0, c == 7)
                           for c in range(8)], t_w, *bank_free[b])
                jj = 4 * (n % 2) + j
                t_sg[n // 2, jj] = act(dst[:, jj, :], ps[b][:, 0:256], ACT.Sigmoid, tok, t_x4[7], t_h5[7])
                bank_free[b] = [t_sg[n // 2, jj]]
            if half:
                free(key, tok)

        for s in range(10):
            if s < 8:
                p[s] = scores(s)
            if 1 <= s <= 8:
                a_[s - 1] = suffix(s - 1, p[s - 1])
            if s < 8:
                gates(s // 2, s % 2)
            if 1 <= s <= 8:
                values(s - 1, a_[s - 1])
            some_taps(10)
        some_taps(1000)

        fence = all_last()
        TMP = A(6144, 4, 256)
        MU = A(6144 + 1024, 256)
        RS = A(6144 + 1280, 256)
        t_m = mean_pe(0, 0, CA, inv512, [t_tap[j] for j in range(4)])
        t_xc = []
        for j in range(4):
            t_xc.append(tt(CA[:, j, :], CA[:, j, :], ps[0][:, 0:256], SUB, t_m))
        bank_free[0] = [t_xc[3]]
        wait("act", fence)
        wait("dve", fence)
        t_s = [act(TMP[:, j, :], CA[:, j, :], ACT.Square, t_xc[j]) for j in range(4)]
        t_m = mean_pe(1, 0, TMP, inv512, t_s)
        t_rs = rsqrt(RS, ps[1][:, 0:256], t_m)
        bank_free[1] = [t_rs]
        t_cs = []
        for j in range(4):
            a = tt(CA[:, j, :], CA[:, j, :], RS, M, t_rs)
            t_cs.append(act(CA[:, j, :], CA[:, j, :], ACT.Silu, a, scale=vcol("ln_g", j), bias=vcol("ln_b", j)))
        MG = A(10240, 8, 256)
        wc, t_wc = slot(("cb", 0))
        wc = wc.rearrange("p (c n) -> p c n", c=4)
        wa, t_wa = slot(("ab", 0))
        wa = wa.rearrange("p (c n) -> p c n", c=4)
        t_ma = []
        for j in range(8):
            b = 2 + j % 3
            tok = mms([(ps[b][:, 0:256], wa[:, c, j * 128:j * 128 + 128], AT[:, c, :], c == 0, c == 3)
                       for c in range(4)], t_wa, *t_attT, *bank_free[b])
            a = tt(SGA[:, j, :], SGA[:, j, :], ps[b][:, 0:256], M, tok, t_sg[1, j])
            bank_free[b] = [a]
            t_ma.append(a)
        free(("ab", 0), tok)
        t_mg = []
        for j in range(8):
            b = 5 + j % 3
            tok = mms([(ps[b][:, 0:256], wc[:, c, j * 128:j * 128 + 128], CA[:, c, :], c == 0, c == 3)
                       for c in range(4)], t_wc, *t_cs, *bank_free[b])
            a = stt(SGC[:, j, :], ps[b][:, 0:256], vcol("b_cb", j), SGC[:, j, :], ADD, M, tok, t_sg[0, j])
            bank_free[b] = [a]
            t_mg.append(tt(MG[:, j, :], SGC[:, j, :], SGA[:, j, :], ADD, a, t_ma[j]))
        free(("cb", 0), tok)
        MX = A(2048, 8, 256)
        SQ = A(4096, 8, 256)
        fence = all_last()
        wait("act", fence)
        t_mx, t_sq = [], []

        for n in range(2):
            def ev(j, p, tok, n=n):
                jj = 4 * n + j
                t_sq.append(act(SQ[:, jj, :], p, ACT.Square, tok))
                t_mx.append(act(MX[:, jj, :], p, ACT.Copy, tok, t_vec, scale=vcol("post2", jj)))
                return [t_mx[-1]]
            free(("out2", n), project(("out2", n), 4, MG, t_mg, ev, [0, 1, 2, 3]))
        t_m = mean_pe(4, 0, SQ, inv1024, t_sq)
        R6 = A(o + 512, 256)
        R7 = A(o + 768, 256)
        t_r6 = rsqrt(R6, ps[4][:, 0:256], t_m)
        bank_free[4] = [t_r6]
        XG = A(6144, 8, 256)
        t_x5, t_xg, t_sq = [], [], []
        for j in range(8):
            a = tt(MX[:, j, :], MX[:, j, :], R6, M, t_r6, t_mx[j])
            a = tt(XT[:, j, :], XT[:, j, :], MX[:, j, :], ADD, a)
            t_x5.append(a)
            t_xg.append(act(XG[:, j, :], XT[:, j, :], ACT.Copy, a, scale=vcol("fpre2", j)))
            t_sq.append(act(SQ[:, j, :], XT[:, j, :], ACT.Square, a, t_m))
        H7 = A(2048, 8, 256)
        FF = A(8192, 22, 256)
        TG = A(13824, 4, 256)
        R7 = A(14848, 256)
        GB = A(15104, 1024)
        SM2 = A(16128, 8)
        fence = all_last()
        wait("act", fence)
        t_gb = load("act", GB, dr["gpost"].partition_broadcast(128), sem("l_gb"))
        fb = [0, 1, 2, 3, 4, 5, 6]
        ix = [0]
        t_ff = []
        t_r7 = None
        t_tg = {}
        for s in range(11):
            w, t_w = slot(("fup", s))
            w = w.rearrange("p (c n) -> p c n", c=8)
            src, t_src = (XG, t_xg) if s == 0 else (H7, t_h7)
            pend = []
            for j in range(2):
                bs = []
                for z in range(2):
                    b = fb[ix[0] % 7]
                    ix[0] += 1
                    wait("pe", bank_free[b])
                    for c in range(8):
                        at = z * 256 + j * 128
                        tok = mms([(ps[b][:, 0:256], w[:, c, at:at + 128], src[:, c, :], c == 0, c == 7)], t_w,
                                  t_src[c])
                    bs.append((b, tok))
                pend.append((2 * s + j, bs))
                if s == 0 and j == 0:
                    t_m = mean_pe(7, 0, SQ, inv1024, t_sq)
                    t_r7 = rsqrt(R7, ps[7][:, 0:256], t_m, *fence)
                    bank_free[7] = [t_r7]
                    t_h7 = [tt(H7[:, c, :], XG[:, c, :], R7, M, t_r7, t_xg[c]) for c in range(8)]
            free(("fup", s), tok)
            for jj, ((b0, k0), (b1, k1)) in pend:
                g = TG[:, jj % 2, :]
                u = TG[:, 2 + jj % 2, :]
                old = [t_ff[jj - 2]] if jj >= 2 else []
                if s == 0:
                    a = tt(g, ps[b0][:, 0:256], R7, M, k0, t_r7, *old)
                    bank_free[b0] = [a]
                    a = act(g, g, ACT.Silu, a)
                    bb = tt(u, ps[b1][:, 0:256], R7, M, k1, t_r7)
                    bank_free[b1] = [bb]
                    t_ff.append(tt(FF[:, jj, :], g, u, M, a, bb, *fence))
                else:
                    a = act(g, ps[b0][:, 0:256], ACT.Silu, k0, *old)
                    bank_free[b0] = [a]
                    t_ff.append(tt(FF[:, jj, :], ps[b1][:, 0:256], g, M, a, k1))
                    bank_free[b1] = [t_ff[-1]]
            if s == 4:
                X5 = A(4096, 2, 1024)
                t_x5k = []
                for i in range(2):
                    for q in range(2):
                        b = fb[ix[0] % 7]
                        ix[0] += 1
                        tok = tts([(ps[b][:, c * 128:c * 128 + 128], XT[:, 4 * q + c, i * 128:i * 128 + 128])
                                   for c in range(4)], ident, *t_x5, *bank_free[b])
                        k = act(X5[:, i, q * 512:q * 512 + 512], ps[b][:, :], ACT.Copy, tok, t_m)
                        bank_free[b] = [k]
                        t_x5k.append(k)
        s_out = sem("s_out")
        OUT = XG
        OUT = A(6144, 2, 1024)
        SCR = A(2048, 2, 1024)
        t_lastup = tok
        for i in range(2):
            ss = SM2[:, 2 * i:2 * i + 2]
            t = []
            for n in range(2):
                wait("pe", bank_free[2 * i + n])
            for k in range(22):
                w, t_w = slot(("fdn", k // 4))
                w = w.rearrange("p (c n) -> p c n", c=4)
                for n in range(2):
                    tok = mms([(ps[2 * i + n][:, :], FF[:, k, i * 128:i * 128 + 128],
                                w[:, k % 4, n * 512:n * 512 + 512], k == 0, k == 21)], t_w, t_ff[k])
                if i == 1 and k % 4 == 3 or k == 21:
                    free(("fdn", k // 4), tok)
            for n in range(2):
                t.append(act(SCR[:, i, n * 512:n * 512 + 512], ps[2 * i + n][:, :], ACT.Square, tok, t_lastup,
                             scale=1.0 / 32, accum_out=ss[:, n:n + 1]))
            rr = SM2[:, 4 + i:5 + i]
            a = tt(rr, ss[:, 0:1], ss[:, 1:2], ADD, *t)
            a = rsqrt(rr, rr, a)
            for n in range(2):
                sl = slice(n * 512, n * 512 + 512)
                k = stt(OUT[:, i, sl], ps[2 * i + n][:, :], rr, GB[:, sl], M, M, a, t_gb, t_lastup)
                k = tt(OUT[:, i, sl], OUT[:, i, sl], X5[:, i, sl], ADD, k, *t_x5k)
                load("act", out_ap[0, i * 128:i * 128 + 128, sl], OUT[:, i, sl], s_out, k)
        wait("act", [(s_out, 64)])

        src_of = {"in1": "w_in", "out1": "w_out", "pproj": "w_pp", "pgate": "w_pg", "in2": "w_in2", "cb": "w_cb",
                  "ab": "w_ab", "out2": "w_out2", "fup": "w_up2", "fdn": "w_dn2"}
        for i, (name, n) in enumerate(order):
            src = dr["moe"][i - 8] if name in "gud" else dr[src_of[name]][n]
            if (name, n) == ("fdn", 5):
                src = src[:, 0:2048]
            dst = ring[:, i % RING, 0:src.shape[1]]
            wait("sp", [freed[i - RING]] if i >= RING else [])
            queue["sp"].append(lambda e, dst=dst, src=src, i=i: e.dma_start(dst, src).then_inc(ring_sem[i % RING], 16))

        block = ctx.enter_context(nc.Block())

        @block.tensor
        def _(e):
            for f in queue["pe"]:
                f(e)

        @block.vector
        def _(e):
            for f in queue["dve"]:
                f(e)

        @block.scalar
        def _(e):
            for f in queue["act"]:
                f(e)

        @block.gpsimd
        def _(e):
            for f in queue["pool"]:
                f(e)

        @block.sync
        def _(e):
            for f in queue["sp"]:
                f(e)


def _cols(a, n):
    k = a.shape[0]
    w = a.shape[1] // n
    return np.ascontiguousarray(a.reshape(k // 128, 128, n, w).transpose(2, 1, 0, 3)).reshape(n, 128, -1)


def _feat(v):
    return v.reshape(-1, 128).T


def _layout(i):
    r = {}
    x = i["x"][0]
    r["x"] = np.ascontiguousarray(x.reshape(2, 128, 1024).transpose(1, 0, 2))
    r["xT"] = np.ascontiguousarray(x.T.reshape(8, 128, 256).transpose(1, 0, 2))
    r["pT"] = np.ascontiguousarray(i["p"][0, 0].T.reshape(2, 128, 256).transpose(1, 0, 2))
    w = i["w_in"][0]
    r["w_in"] = _cols(np.concatenate([w[:, 2048:], w[:, 1536:2048], w[:, 512:1024], w[:, 1024:1536], w[:, :512]], 1), 5)
    r["w_out"] = _cols(i["w_out"][0], 2)
    pp = i["w_ple_proj"][0]
    r["w_pp"] = _cols(pp, 1)
    r["w_pg"] = _cols(i["w_ple_gate"][0], 2)
    g, u, d = (i[k][0].reshape((NE,) + i[k].shape[3:]) for k in ("w_gate", "w_up", "w_down"))
    src = {"g": g, "u": u, "d": d}
    moe = np.empty((96, 128, SLOT), g.dtype)
    for n, (k, e) in enumerate(moe_order()):
        moe[n] = _cols(src[k][e], 1)[0]
    r["moe"] = moe
    w = i["w_in_2"]
    r["w_in2"] = _cols(np.concatenate([w[:, 512:1024], w[:, 0:512], w[:, 1024:]], 1), 9)
    r["w_cb"] = _cols(i["w_conv_branch_2"], 1)
    r["w_ab"] = _cols(i["w_att_branch_2"], 1)
    r["w_out2"] = _cols(i["w_out_2"], 2)
    w = i["w_ffn_up_2"].reshape(1024, 2, 11, 256).transpose(0, 2, 1, 3).reshape(1024, 5632)
    r["w_up2"] = _cols(w, 11)
    dn = i["w_ffn_down_2"]
    dn = np.concatenate([dn, dn[:256]], 0)
    r["w_dn2"] = np.ascontiguousarray(dn.reshape(6, 4, 128, 1024).transpose(0, 2, 1, 3)).reshape(6, 128, SLOT)
    wr = np.concatenate([i["w_group"][0], i["w_router"][0].transpose(1, 0, 2).reshape(1024, 32)], 1)
    r["wr"] = np.ascontiguousarray(wr.reshape(8, 128, 36).transpose(1, 0, 2))
    r["lbias"] = np.concatenate([i["b_group"][0], i["b_router"][0].reshape(-1)])[None]
    r["wsT"] = np.ascontiguousarray(i["w_spatial"][0].transpose(2, 0, 1)).reshape(128, 1024)
    r["b_sp"] = np.ascontiguousarray(i["b_spatial"][0].reshape(4, 2, 128).transpose(1, 0, 2))
    r["gpost"] = i["norm_ffn_post_2"][None]
    v = [_feat(i["g_mix"][0]), i["w_conv"][0].reshape(12, 128).T, _feat(i["g_sgu"][0]), _feat(i["g_ffn"][0]),
         _feat(i["g_ple"][0]), _feat(i["g_final"]), _feat(i["norm_mix_pre_2"]),
         i["conv_dw_w_2"].reshape(124, 128).T, _feat(i["conv_dw_b_2"]), _feat(i["conv_ln_g_2"]),
         _feat(i["conv_ln_b_2"]), _feat(i["b_conv_branch_2"]), _feat(i["norm_mix_post_2"]),
         _feat(i["norm_ffn_pre_2"])]
    r["vec"] = np.ascontiguousarray(np.concatenate(v, 1))
    c = np.zeros((128, N_CST), np.float32)
    k = np.arange(128)
    c[:, C_ID:C_ID + 128] = np.eye(128)
    c[:, C_U:C_U + 128] = k[:, None] < k[None]
    c[:, C_TRI:C_TRI + 128] = k[:, None] >= k[None]
    nmd = np.where(k[:, None] < k[None], 0.0, -1e30)
    c[:, C_NM:C_NM + 128] = nmd
    c[:, C_NM + 256:C_NM + 384] = nmd
    c[:, C_IOTA:C_IOTA + CAP] = np.arange(CAP)
    c[:, C_IX:C_IX + 8] = np.arange(8) - 64.0
    r["cst"] = c
    return r


def kernel(**inputs):
    import concourse.bacc as bacc
    from concourse.bass_utils import run_bass_kernel_spmd

    nc = bacc.Bacc("TRN2", target_bir_lowering=False, num_devices=1)
    arrays, dr = {}, {}
    for name, a in _layout({k: np.asarray(v) for k, v in inputs.items()}).items():
        a = np.ascontiguousarray(a)
        arrays["in_" + name] = a
        dr[name] = nc.dram_tensor("in_" + name, a.shape, mybir.dt.from_np(a.dtype), kind="ExternalInput").ap()
    out = nc.dram_tensor("out_0", (1, T, D), F32, kind="ExternalOutput").ap()
    build(nc, dr, out)
    r = run_bass_kernel_spmd(nc, [arrays], core_ids=[0])
    return r.results[0]["out_0"]
```

```python
from contextlib import ExitStack

import numpy as np

import concourse.bass as bass
from concourse import mybir

F32 = mybir.dt.float32
I32 = mybir.dt.int32
ALU = mybir.AluOpType
ACT = mybir.ActivationFunctionType
AX = mybir.AxisListType.X

T = 256
D = 1024
NE = 32
CAP = 64
NP = NE // 2
EPS = 1e-6
RING = 8
SLOT = 4096

C_ID, C_U, C_TRI, C_NM, C_IOTA, C_IX = 0, 128, 256, 384, 768, 832
N_CST = 840
VEC = {}
_at = 0
for _n, _w in (("g_mix", 8), ("w_conv", 12), ("g_sgu", 4), ("g_ffn", 8), ("g_ple", 8), ("g_final", 8),
               ("pre2", 8), ("dw_w", 124), ("dw_b", 4), ("ln_g", 4), ("ln_b", 4), ("b_cb", 8), ("post2", 8),
               ("fpre2", 8)):
    VEC[_n] = _at
    _at += _w
N_VEC = _at


def moe_order():
    return [(k, 2 * q + r) for q in range(NP) for k in "gud" for r in range(2)]


def stream():
    out = [("in1", i) for i in range(5)] + [("out1", i) for i in range(2)] + [("pproj", 0)]
    out += moe_order()
    out += [("pgate", i) for i in range(2)] + [("in2", i) for i in range(9)]
    out += [("cb", 0), ("ab", 0)] + [("out2", i) for i in range(2)]
    out += [("fup", i) for i in range(11)] + [("fdn", i) for i in range(6)]
    return out


def build(nc, dr, out_ap):
    ctx = ExitStack()
    with ctx:
        def sem(name):
            return ctx.enter_context(nc.semaphore(name))

        ring = ctx.enter_context(nc.sbuf_tensor("ring", [128, RING, SLOT], F32))
        cst = ctx.enter_context(nc.sbuf_tensor("cst", [128, N_CST], F32))
        vec = ctx.enter_context(nc.sbuf_tensor("vec", [128, N_VEC], F32))
        wr = ctx.enter_context(nc.sbuf_tensor("wr", [128, 8, 36], F32))
        ones = ctx.enter_context(nc.sbuf_tensor("ones", [128, 3, 128], F32))
        flag = ctx.enter_context(nc.sbuf_tensor("flag", [128, 1], I32))
        eps = ctx.enter_context(nc.sbuf_tensor("eps", [128, 1], F32))
        NAR = 18688
        arena = ctx.enter_context(nc.sbuf_tensor("arena", [128, NAR], F32))
        ps = [ctx.enter_context(nc.psum_tensor(f"ps{i}", [128, 512], F32)) for i in range(8)]

        def A(at, *shape):
            n = 1
            for s in shape:
                n *= s
            assert at + n <= NAR, (at, n)
            v = arena[:, at:at + n]
            if len(shape) == 2:
                v = v.rearrange("p (a b) -> p a b", a=shape[0])
            elif len(shape) == 3:
                v = v.rearrange("p (a b c) -> p a b c", a=shape[0], b=shape[1])
            return v

        names = ("pe", "dve", "act", "pool", "sp")
        queue = {n: [] for n in names}
        done_sem = {n: sem("done_" + n) for n in names}
        count = {n: 0 for n in names}
        seen = {n: {} for n in names}

        def wait(eng, toks):
            for tok in toks:
                s, v = tok
                if seen[eng].get(id(s), 0) < v:
                    seen[eng][id(s)] = v
                    queue[eng].append(lambda e, s=s, v=v: e.wait_ge(s, v))

        def op(eng, fn, *toks):
            wait(eng, toks)
            count[eng] += 1
            s = done_sem[eng]
            queue[eng].append(lambda e: fn(e).then_inc(s, 1))
            return (s, count[eng])

        def last(eng):
            return (done_sem[eng], count[eng])

        def all_last():
            return [last(n) for n in ("pe", "dve", "act") if count[n]]

        def load(eng, dst, src, s, *toks):
            wait(eng, toks)
            queue[eng].append(lambda e: e.dma_start(dst, src).then_inc(s, 16))
            return (s, 16)

        def mms(lst, *toks):
            wait("pe", toks)
            for o, l, r, a, z in lst[:-1]:
                queue["pe"].append(lambda e, o=o, l=l, r=r, a=a, z=z: e.matmul(
                    o, l, r, start=a, stop=z, skip_group_check=True))
            o, l, r, a, z = lst[-1]
            return op("pe", lambda e: e.matmul(o, l, r, start=a, stop=z, skip_group_check=True))

        def tts(lst, ident, *toks):
            wait("pe", toks)
            for o, i in lst[:-1]:
                queue["pe"].append(lambda e, o=o, i=i: e.transpose(o, i, ident))
            o, i = lst[-1]
            return op("pe", lambda e: e.transpose(o, i, ident))

        bank_free = [[] for _ in range(8)]

        def tt(o, a, b, f, *toks, eng="dve"):
            return op(eng, lambda e: e.tensor_tensor(o, a, b, f), *toks)

        def ts(o, a, s1, s2, f0, f1, *toks, eng="dve"):
            if f1 is None:
                return op(eng, lambda e: e.tensor_scalar(o, a, s1, s2, f0), *toks)
            return op(eng, lambda e: e.tensor_scalar(o, a, s1, s2, f0, f1), *toks)

        def stt(o, a, s, b, f0, f1, *toks):
            return op("dve", lambda e: e.scalar_tensor_tensor(out=o, in0=a, scalar=s, in1=b, op0=f0, op1=f1), *toks)

        def act(o, a, f, *toks, **kw):
            return op("act", lambda e: e.activation(o, a, f, **kw), *toks)

        def red(o, a, f, *toks):
            return op("dve", lambda e: e.tensor_reduce(o, a, AX, f), *toks)

        M, ADD, SUB, MAX = ALU.mult, ALU.add, ALU.subtract, ALU.max

        order = stream()
        index = {k: i for i, k in enumerate(order)}
        ring_sem = [sem(f"ring{i}") for i in range(RING)]
        freed = {}

        def slot(key):
            i = index[key]
            return ring[:, i % RING, :], (ring_sem[i % RING], 16 * (i // RING + 1))

        def free(key, tok):
            freed[index[key]] = tok

        ident = cst[:, C_ID:C_ID + 128]
        U = cst[:, C_U:C_U + 128]
        tri = cst[:, C_TRI:C_TRI + 128]
        nm = cst[:, C_NM:C_NM + 384]
        iota = cst[:, C_IOTA:C_IOTA + CAP]
        ix8 = cst[:, C_IX:C_IX + 8]
        one, inv1024, inv512 = ones[:, 0, :], ones[:, 1, :], ones[:, 2, :]

        def vcol(name, i):
            return vec[:, VEC[name] + i:VEC[name] + i + 1]

        XT = A(0, 8, 256)
        XK = A(2048, 2, 1024)
        H1 = A(4096, 8, 256)
        MIX = A(6144, 8, 256)
        PP = A(8192, 8, 256)
        SQ = A(10240, 8, 256)
        o = 12288
        VG = A(o, 2, 512)
        UG = A(o + 1024, 4, 256)
        Z = A(o + 2048, 4, 258)
        CR = A(o + 3080, 4, 256)
        PT = A(o + 4104, 2, 256)
        R1B = A(o + 4616, 256)
        BB = A(o + 4872, 4, 128)
        SM = A(o + 5384, 720)
        WS = PP

        t_xT = load("act", XT, dr["xT"], sem("l_xT"))
        t_vec = load("act", vec[:], dr["vec"], sem("l_vec"))
        t_xk = load("act", XK, dr["x"], sem("l_xk"))
        t_cst = load("act", cst[:], dr["cst"], sem("l_cst"))
        t_wr = load("act", wr[:], dr["wr"], sem("l_wr"))
        t_ws = load("act", WS[:, 0:4, :].rearrange("p a b -> p (a b)"), dr["wsT"], sem("l_ws"))
        s_bb = sem("l_bb")
        load("act", BB[0:64], dr["b_sp"][0:1, :, :].partition_broadcast(64), s_bb)
        load("act", BB[64:128], dr["b_sp"][1:2, :, :].partition_broadcast(64), s_bb)
        t_bb = (s_bb, 32)
        t_pT = load("act", PT, dr["pT"], sem("l_pT"))
        LB = SM[:, 0:36]
        t_lb = load("act", LB, dr["lbias"].partition_broadcast(128), sem("l_lb"))

        t_eps = op("dve", lambda e: e.memset(eps[:], EPS))
        op("dve", lambda e: e.memset(ones[:, 0, :], 1.0))
        op("dve", lambda e: e.memset(ones[:, 1, :], 1.0 / 1024))
        t_ones = op("dve", lambda e: e.memset(ones[:, 2, :], 1.0 / 512))
        t_zpad = op("dve", lambda e: e.memset(Z[:, :, 0:2], 0.0))

        def scale_cols(dst, src, name, *toks):
            return [ts(dst[:, c, :], src[:, c, :], vcol(name, c), None, M, None, *toks) for c in range(8)]

        def squares(dst, src, toks):
            return [act(dst[:, c, :], src[:, c, :], ACT.Square, toks[c]) for c in range(len(toks))]

        def mean_pe(bank, at, src, w, toks):
            n = len(toks)
            wait("pe", bank_free[bank])
            for c in range(n):
                tok = mms([(ps[bank][:, at:at + 256], w, src[:, c, :], c == 0, c == n - 1)], toks[c])
            return tok

        def rsqrt(dst, src, *toks):
            a = act(dst, src, ACT.Sqrt, t_eps, *toks, bias=eps[:, 0:1])
            return op("dve", lambda e: e.reciprocal(dst, dst), a)

        XG = SQ
        t_xg = scale_cols(XG, XT, "g_mix", t_xT, t_vec)
        SQ0 = MIX
        t_sq = squares(SQ0, XT, [t_xT] * 8)
        RT = SM[:, 40:42]
        for i in range(2):
            t_rt = act(VG.rearrange("p a b -> p (a b)"), XK[:, i, :], ACT.Square, t_xk, last("act"), scale=1.0 / 32,
                       accum_out=RT[:, i:i + 1])
        t_rt = rsqrt(RT, RT, t_rt)

        w, t_w = slot(("in1", 0))
        w = w.rearrange("p (c n) -> p c n", c=8)
        t_v = []
        for i in range(2):
            for c in range(8):
                tok = mms([(ps[i][:, :], XG[:, c, i * 128:i * 128 + 128], w[:, c, :], c == 0, c == 7)], t_w, t_xg[c])
            t_v.append(tok)
            if i == 0:
                wait("pe", [t_ones])
                t_m = mean_pe(2, 0, SQ0, inv1024, t_sq)
        free(("in1", 0), t_v[1])
        t_r1b = rsqrt(R1B, ps[2][:, 0:256], t_m)
        bank_free[2] = [t_r1b]
        t_h1 = [tt(H1[:, c, :], XG[:, c, :], R1B, M, t_r1b, t_xg[c]) for c in range(8)]
        VS = SM[:, 42:44]
        VM = SM[:, 44:46]
        t_g = []
        for i in range(2):
            t_g.append(act(VG[:, i, :], ps[i][:, :], ACT.Gelu_apprx_tanh, t_v[i], t_rt, scale=RT[:, i:i + 1],
                           accum_out=VS[:, i:i + 1]))
            bank_free[i] = [t_g[i]]
        t = ts(VM, VS, -1.0 / 512, None, M, None, t_g[1])
        t_xc = [ts(VG[:, i, :], VG[:, i, :], VM[:, i:i + 1], None, ADD, None, t, t_g[i]) for i in range(2)]
        VV = SM[:, 46:48]
        for i in range(2):
            t = act(SM[:, 200:712], VG[:, i, :], ACT.Square, t_xc[i], last("act"), accum_out=VV[:, i:i + 1])
        t = ts(VV, VV, 1.0 / 512, None, M, None, t)
        t = rsqrt(VV, VV, t)
        t_vn = [ts(VG[:, i, :], VG[:, i, :], VV[:, i:i + 1], None, M, None, t) for i in range(2)]

        def project(key, n_out, src, t_src, evac, banks, c_n=8, at=0):
            w, t_w = slot(key)
            w = w.rearrange("p (c n) -> p c n", c=c_n)
            for j in range(n_out):
                b = banks[j % len(banks)]
                wait("pe", bank_free[b])
                for c in range(c_n):
                    tok = mms([(ps[b][:, 0:256], w[:, c, at + j * 128:at + j * 128 + 128], src[:, c, :],
                                c == 0, c == c_n - 1)], t_w, t_src[c])
                bank_free[b] = evac(j, ps[b][:, 0:256], tok)
            return tok

        t_u = []

        def ev_u(j, p, tok):
            t_u.append(act(UG[:, j, :], p, ACT.Gelu_apprx_tanh, tok))
            return [t_u[-1]]

        free(("in1", 1), project(("in1", 1), 4, H1, t_h1, ev_u, [3, 4, 5, 6]))
        t_c = []

        def ev_c(j, p, tok):
            t_c.append(act(CR[:, j, :], p, ACT.Copy, tok))
            return [t_c[-1]]

        free(("in1", 2), project(("in1", 2), 4, H1, t_h1, ev_c, [0, 1, 2, 7]))
        t_cv = []

        def ev_x(j, p, tok):
            z = Z[:, j, 2:258]
            a = tt(z, p, CR[:, j, :], M, tok, t_c[j], t_zpad)
            k = ts(CR[:, j, :], z, vcol("w_conv", 8 + j), None, M, None, a)
            k = stt(CR[:, j, :], Z[:, j, 1:257], vcol("w_conv", 4 + j), CR[:, j, :], M, ADD, k)
            t_cv.append(stt(CR[:, j, :], Z[:, j, 0:256], vcol("w_conv", j), CR[:, j, :], M, ADD, k))
            return [a]

        free(("in1", 3), project(("in1", 3), 4, H1, t_h1, ev_x, [3, 4, 5, 6]))
        t_mix = []

        def ev_b(j, p, tok):
            t_mix.append(tt(MIX[:, j, :], p, CR[:, j, :], M, tok, t_cv[j], t_m))
            return [t_mix[-1]]

        free(("in1", 4), project(("in1", 4), 4, H1, t_h1, ev_b, [0, 1, 2, 7]))
        wsv = WS[:, 0:4, :].rearrange("p a (h t) -> p (a h) t", h=2)
        t_msk = op("pool", lambda e: e.affine_select(
            out=wsv, in_=wsv, compare_op=ALU.is_ge, fill=0.0, base=0, pattern=[[0, 8], [1, 128]],
            channel_multiplier=-1), t_ws)
        t_s = []
        for j in range(4):
            b = 3 + j
            wait("pe", bank_free[b] + [t_msk] + t_vn)
            lst = []
            for hh in range(2):
                h = 2 * j + hh
                for i in range(2):
                    lst.append((ps[b][64 * hh:64 * hh + 64, i * 128:i * 128 + 128], VG[:, i, h * 64:h * 64 + 64],
                                wsv[:, h, :], i == 0, True))
            tok = mms(lst)
            mx = MIX[:, 4 + j, :].rearrange("p (i t) -> p i t", i=2)
            k = None
            for i in range(2):
                k = stt(mx[:, i, :], ps[b][:, i * 128:i * 128 + 128], vcol("g_sgu", j), BB[:, j, :], M, ADD, tok, t_bb,
                        t_m)
            bank_free[b] = [k]
            t_mix.append(tt(MIX[:, 4 + j, :], MIX[:, 4 + j, :], UG[:, j, :], M, k, t_u[j]))
        t_x1 = {}
        for n in range(2):
            w, t_w = slot(("out1", n))
            w = w.rearrange("p (c n) -> p c n", c=8)
            for i in range(2):
                b = [0, 1, 2, 7][2 * n + i]
                wait("pe", bank_free[b])
                for c in range(8):
                    tok = mms([(ps[b][:, :], MIX[:, c, i * 128:i * 128 + 128], w[:, c, :], c == 0, c == 7)],
                              t_w, t_mix[c])
                x = XK[:, i, n * 512:n * 512 + 512]
                t_x1[i, n] = tt(x, x, ps[b][:, :], ADD, tok, t_xk)
                bank_free[b] = [t_x1[i, n]]
            free(("out1", n), tok)
        t_x1a = t_x1[1, 1]
        R2 = SM[:, 48:50]
        for i in range(2):
            t = act(SQ[:, 0:4, :].rearrange("p a b -> p (a b)"), XK[:, i, :], ACT.Square, t_x1a, last("act"), last("pe"),
                    scale=1.0 / 32, accum_out=R2[:, i:i + 1])
        t_r2 = rsqrt(R2, R2, t)
        t_wrg = None
        for c in range(8):
            t_wrg = ts(wr[:, c, :], wr[:, c, :], vcol("g_ffn", c), None, M, None, t_wr)
        t_xT1 = []
        for q in range(4):
            b = 3 + q
            tok = tts([(ps[b][:, (cc * 2 + i) * 128:(cc * 2 + i) * 128 + 128],
                        XK[:, i, (2 * q + cc) * 128:(2 * q + cc) * 128 + 128]) for cc in range(2) for i in range(2)],
                      ident, t_x1a, t_cst, *bank_free[b])
            dst = XT[:, 2 * q:2 * q + 2, :].rearrange("p a b -> p (a b)")
            if q % 2:
                k = act(dst, ps[b][:, :], ACT.Copy, tok)
            else:
                k = op("dve", lambda e, dst=dst, b=b: e.tensor_copy(dst, ps[b][:, :]), tok)
            bank_free[b] = [k]
            t_xT1 += [k, k]
        wait("pe", [t_wrg] + bank_free[0] + bank_free[1])
        for i in range(2):
            for c in range(8):
                tok = mms([(ps[i][:, 0:36], XT[:, c, i * 128:i * 128 + 128], wr[:, c, :], c == 0, c == 7)], t_xT1[c])
        t_lg = tok
        X1H = H1
        t_x1h = [act(X1H[:, :, :].rearrange("p a b -> p (a b)")[:, i * 1024:i * 1024 + 1024], XK[:, i, :], ACT.Copy,
                     t_r2, scale=R2[:, i:i + 1]) for i in range(2)]
        x1h = A(4096, 2, 1024)
        t_pp = []
        w, t_w = slot(("pproj", 0))
        w = w.rearrange("p (c n) -> p c n", c=4)
        for j in range(8):
            b = [2, 7, 3, 4][j % 4]
            tok = mms([(ps[b][:, 0:256], w[:, c, j * 128:j * 128 + 128], PT[:, c, :], c == 0, c == 1)
                       for c in range(2)], t_w, t_pT, *bank_free[b])
            k = act(PP[:, j, :], ps[b][:, 0:256], ACT.Copy, tok, last("pe"))
            bank_free[b] = [k]
            t_pp.append(k)
        free(("pproj", 0), tok)

        q = [50]

        def small(n):
            v = SM[:, q[0]:q[0] + n]
            q[0] += n
            assert q[0] <= 720
            return v

        LG = small(72).rearrange("p (i n) -> p i n", i=2)
        for i in range(2):
            t = stt(LG[:, i, :], ps[i][:, 0:36], R2[:, i:i + 1], LB, M, ADD, t_lg, t_r2, t_lb)
            bank_free[i] = [t]
        GL = LG[:, :, 0:4]
        EL = LG[:, :, 4:36].rearrange("p i (g e) -> p i g e", g=4)

        def first_max(src, n, t):
            mx = small(2)
            eq = small(2 * n).rearrange("p (i n) -> p i n", i=2)
            mn = small(2)
            t = red(mx, src, ALU.max, t)
            tm = t
            t = tt(eq, src, mx.unsqueeze(2).to_broadcast([128, 2, n]), ALU.is_equal, t)
            t = tt(eq, eq, ix8[:, 0:n].unsqueeze(1).to_broadcast([128, 2, n]), M, t, t_cst)
            t = red(mn, eq, ALU.min, t)
            t = tt(eq, ix8[:, 0:n].unsqueeze(1).to_broadcast([128, 2, n]), mn.unsqueeze(2).to_broadcast([128, 2, n]),
                   ALU.is_equal, t)
            return mx, eq, tm, t

        gm, goh, tm, t_goh = first_max(GL, 4, t)
        ngm = small(2)
        t = ts(ngm, gm, -1.0, None, M, None, tm)
        gex = small(8).rearrange("p (i n) -> p i n", i=2)
        gs = small(2)
        for i in range(2):
            t_gs = act(gex[:, i, :], GL[:, i, :], ACT.Exp, t, bias=ngm[:, i:i + 1], accum_out=gs[:, i:i + 1])
        em = small(64).rearrange("p (i g e) -> p i g e", i=2, g=4)
        t = None
        for i in range(2):
            t = tt(em[:, i], EL[:, i], goh[:, i, :].unsqueeze(2).to_broadcast([128, 4, 8]), M, t_goh)
        es = small(16).rearrange("p (i e) -> p i e", i=2)
        for i in range(2):
            tr = red(es[:, i, :], em[:, i].rearrange("p g e -> p e g"), ALU.add, t)
        v1, oh1, _, t1 = first_max(es, 8, tr)
        e2 = small(16).rearrange("p (i e) -> p i e", i=2)
        t = stt(e2, oh1, -1e30, es, M, ADD, t1)
        v2, oh2, _, t2 = first_max(e2, 8, t)
        dv = small(2)
        t = tt(dv, v2, v1, SUB, t2)
        ex = small(2)
        t_ex = act(ex, dv, ACT.Exp, t)
        den = small(2)
        t = ts(den, ex, 1.0, None, ADD, None, t_ex)
        t = tt(den, den, gs, M, t, t_gs)
        w1 = small(2)
        t = op("dve", lambda e: e.reciprocal(w1, den), t)
        w2 = small(2)
        t = tt(w2, w1, ex, M, t)
        inn = small(16).rearrange("p (i e) -> p i e", i=2)
        inb = small(16).rearrange("p (i e) -> p i e", i=2)
        for i in range(2):
            k = ts(inn[:, i, :], oh1[:, i, :], w1[:, i:i + 1], None, M, None, t)
        for i in range(2):
            t = stt(inn[:, i, :], oh2[:, i, :], w2[:, i:i + 1], inn[:, i, :], M, ADD, k)
        k = tt(inb, oh1, oh2, ADD, t2)
        comb = small(64).rearrange("p (i g e) -> p i g e", i=2, g=4)
        mask = small(64).rearrange("p (i g e) -> p i g e", i=2, g=4)
        for i in range(2):
            gb = goh[:, i, :].unsqueeze(2).to_broadcast([128, 4, 8])
            t_mk = tt(mask[:, i], inb[:, i, :].unsqueeze(1).to_broadcast([128, 4, 8]), gb, M, k)
            t_cb = tt(comb[:, i], inn[:, i, :].unsqueeze(1).to_broadcast([128, 4, 8]), gb, M, t)
        mk = mask.rearrange("p i g e -> p i (g e)")
        cb = comb.rearrange("p i g e -> p i (g e)")
        wait("pe", bank_free[0] + bank_free[1] + [t_mk])
        t_pos = mms([(ps[0][:, 0:32], U, mk[:, 0, :], True, True),
                     (ps[0][:, 32:64], U, mk[:, 1, :], True, False),
                     (ps[0][:, 32:64], one, mk[:, 0, :], False, True),
                     (ps[0][:, 64:96], one, mk[:, 0, :], True, False),
                     (ps[0][:, 64:96], one, mk[:, 1, :], False, True)])
        pos = small(64).rearrange("p (i e) -> p i e", i=2)
        t = stt(pos, ps[0][:, 0:64].rearrange("p (i e) -> p i e", i=2), 1.0, mk, ADD, M, t_pos)
        t_ps = ts(pos, pos, -1.0, None, ADD, None, t)
        cm = small(1)
        t = red(cm, ps[0][:, 64:96], ALU.max, t_pos)
        bank_free[0] = [t]
        t_flag = ts(flag[:], cm, float(CAP), None, ALU.is_gt, None, t)

        o = 12288
        YS = A(2048, 1024)
        SB = [A(o + 256 * k, 2, 2, CAP) for k in range(2)]
        SC = A(o + 512, 2, 2, CAP)
        SCT = [A(o + 768 + 256 * k, 256) for k in range(2)]
        SG = A(o + 1280, 512)
        HD = A(o + 1792, 512)
        HT = A(o + 2304, 4, 128)
        HC = [A(6144 + 1024 * k, 8, 2 * CAP) for k in range(2)]
        assert o + 2816 <= o + 4104
        fence = all_last()
        for n in ("dve", "act", "pe"):
            wait(n, fence)
        t_hc, t_sct, t_gat, t_gu, t_scat, t_ys, t_htr, t_dn, t_ht = ({} for _ in range(9))
        t_ctr = {}

        def after(d, k):
            return [d[k]] if k in d else []

        def gather(q):
            k = q % 2
            e0 = 2 * q
            for i in range(2):
                io = iota.unsqueeze(1).to_broadcast([128, 2, CAP])
                pb = pos[:, i, e0:e0 + 2].unsqueeze(2).to_broadcast([128, 2, CAP])
                t = tt(SB[k][:, i], io, pb, ALU.is_equal, t_ps, *after(t_gat, q - 2))
            for i in range(2):
                c2 = cb[:, i, e0:e0 + 2].unsqueeze(2).to_broadcast([128, 2, CAP])
                tc = tt(SC[:, i], SB[k][:, i], c2, M, t, t_cb, *after(t_ctr, q - 1))
            for z in range(2):
                bk = 2 + z
                lst = []
                for c in range(4):
                    for i in range(2):
                        lst.append((ps[bk][:, c * 128:c * 128 + 128],
                                    x1h[:, i, (4 * z + c) * 128:(4 * z + c) * 128 + 128],
                                    SB[k][:, i].rearrange("p e s -> p (e s)"), i == 0, i == 1))
                tok = mms(lst, t, *t_x1h, *bank_free[bk])
                g = vec[:, VEC["g_ffn"] + 4 * z:VEC["g_ffn"] + 4 * z + 4].unsqueeze(2).to_broadcast([128, 4, 128])
                t_hc[q] = tt(HC[k][:, 4 * z:4 * z + 4, :], ps[bk][:, :].rearrange("p (c s) -> p c s", c=4), g,
                             M, tok, *after(t_gu, q - 2))
                bank_free[bk] = [t_hc[q]]
            t_gat[q] = tok
            t_ctr[q] = tts([(ps[4][:, i * 128:i * 128 + 128], SC[:, i].rearrange("p e s -> p (e s)"))
                            for i in range(2)], ident, tc, *bank_free[4])
            t_sct[q] = act(SCT[k], ps[4][:, 0:256], ACT.Copy, t_ctr[q], *after(t_scat, q - 2))
            bank_free[4] = [t_sct[q]]

        def gate_up(q):
            hc = HC[q % 2]
            for bk, key in ((0, "g"), (1, "u")):
                ws = [slot((key, 2 * q + r)) for r in range(2)]
                wv = [w_.rearrange("p (c n) -> p c n", c=8) for w_, _ in ws]
                lst = [(ps[bk][64 * r:64 * r + 64, :], hc[:, c, 64 * r:64 * r + 64], wv[r][:, c, :], c == 0, c == 7)
                       for c in range(8) for r in range(2)]
                tok = mms(lst, ws[0][1], ws[1][1], t_hc[q], *bank_free[bk])
                free((key, 2 * q), tok)
                free((key, 2 * q + 1), tok)
                if key == "g":
                    s = act(SG, ps[0][:, :], ACT.Silu, tok, *after(t_h, q - 1))
                    bank_free[0] = [s]
            t_gu[q] = tok
            t_h[q] = tt(HD, ps[1][:, :], SG, M, s, tok, *after(t_htr, q - 1))
            bank_free[1] = [t_h[q]]

        t_h = {}

        def down(q):
            t_htr[q] = tts([(ps[4][:, f * 128:f * 128 + 128], HD[:, f * 128:f * 128 + 128]) for f in range(4)], ident,
                           t_h[q], *bank_free[4])
            t_ht[q] = act(HT.rearrange("p a b -> p (a b)"), ps[4][:, :], ACT.Copy, t_htr[q], *after(t_dn, q - 1))
            bank_free[4] = [t_ht[q]]
            ws = [slot(("d", 2 * q + r)) for r in range(2)]
            wv = [w_.rearrange("p (c n) -> p c n", c=4) for w_, _ in ws]
            t_ys[q] = []
            for n in range(2):
                bk = 5 + n
                lst = [(ps[bk][64 * r:64 * r + 64, :], HT[:, f, 64 * r:64 * r + 64],
                        wv[r][:, f, n * 512:n * 512 + 512], f == 0, f == 3) for f in range(4) for r in range(2)]
                tok = mms(lst, ws[0][1], ws[1][1], t_ht[q], *bank_free[bk])
                k = act(YS[:, n * 512:n * 512 + 512], ps[bk][:, :], ACT.Copy, tok, *after(t_scat, q - 1))
                bank_free[bk] = [k]
                t_ys[q].append(k)
            free(("d", 2 * q), tok)
            free(("d", 2 * q + 1), tok)
            t_dn[q] = tok

        t_acc = {j: t_xT1[2 * j] for j in range(4)}

        def scatter(q):
            for z in range(4):
                bk = [7, 5, 6, 7][z]
                tok = mms([(ps[bk][:, y * 256:y * 256 + 256], YS[:, (2 * z + y) * 128:(2 * z + y) * 128 + 128],
                            SCT[q % 2], True, True) for y in range(2)], t_ys[q][z // 2], t_sct[q], *bank_free[bk])
                x = XT[:, 2 * z:2 * z + 2, :].rearrange("p a b -> p (a b)")
                t_acc[z] = tt(x, x, ps[bk][:, :], ADD, tok, t_acc[z])
                bank_free[bk] = [t_acc[z]]
            t_scat[q] = tok

        gather(0)
        for q in range(NP):
            gate_up(q)
            if q:
                scatter(q - 1)
            if q + 1 < NP:
                gather(q + 1)
            down(q)
        scatter(NP - 1)

        fence = all_last()
        HO = A(10240, 8, 256)
        WG = [A(2048 + 1024 * k, 8, 128) for k in range(2)]
        OH = A(6144, 4, 256)
        WD = A(6144 + 1024, 4, 128)
        OS = A(6144 + 1536, 256)
        CO = A(o, 2, 32)
        COT = A(o + 64, 256)
        s_over = {n: sem("over_" + n) for n in ("pe", "dve", "act", "dma")}
        over = {n: [] for n in names}
        ocnt = {n: 0 for n in s_over}

        def oop(eng, fn, *toks):
            for s, v in toks:
                over[eng].append(lambda e, s=s, v=v: e.wait_ge(s, v))
            ocnt[eng] += 1
            over[eng].append(lambda e: fn(e).then_inc(s_over[eng], 1))
            return (s_over[eng], ocnt[eng])

        def oload(dst, src, *toks):
            for s, v in toks:
                over["pool"].append(lambda e, s=s, v=v: e.wait_ge(s, v))
            ocnt["dma"] += 16
            over["pool"].append(lambda e: e.dma_start(dst, src).then_inc(s_over["dma"], 16))
            return (s_over["dma"], ocnt["dma"])

        def omm(lst, *toks):
            for s, v in toks:
                over["pe"].append(lambda e, s=s, v=v: e.wait_ge(s, v))
            for o_, l, r, a, z in lst[:-1]:
                over["pe"].append(lambda e, o_=o_, l=l, r=r, a=a, z=z: e.matmul(
                    o_, l, r, start=a, stop=z, skip_group_check=True))
            o_, l, r, a, z = lst[-1]
            return oop("pe", lambda e: e.matmul(o_, l, r, start=a, stop=z, skip_group_check=True))

        t = None
        for c in range(8):
            for i in range(2):
                tp = oop("pe", lambda e, c=c, i=i: e.transpose(
                    ps[0][:, i * 128:i * 128 + 128], x1h[:, i, c * 128:c * 128 + 128], ident), *([t] if t else []))
            t = oop("dve", lambda e, c=c: e.tensor_scalar(HO[:, c, :], ps[0][:, 0:256], vcol("g_ffn", c), None, M), tp)
        k = oop("dve", lambda e: e.tensor_scalar(CO, pos, float(CAP) - 0.5, None, ALU.is_ge))
        k = oop("dve", lambda e: e.tensor_tensor(CO, CO, cb, M), k)
        for i in range(2):
            tp = oop("pe", lambda e, i=i: e.transpose(ps[0][0:32, i * 128:i * 128 + 128], CO[:, i, :], ident), k, t)
        t_ready = oop("dve", lambda e: e.tensor_copy(COT[0:32, :], ps[0][0:32, 0:256]), tp)
        t_od = t_ready
        t_wfree = t_dfree = None
        for x in range(NE):
            tb = omm([(ps[1][:, 0:256], ident[0:32, x:x + 1].to_broadcast([32, 128]), COT[0:32, :], True, True)],
                     t_od, t_ready)
            for j in range(4):
                tl = None
                for z, key in enumerate(("g", "u")):
                    src = dr["moe"][index[(key, x)] - 8].rearrange("p (c n) -> p c n", c=8)[:, :, j * 128:j * 128 + 128]
                    tl = oload(WG[z], src, *([t_wfree] if t_wfree else []))
                for z in range(2):
                    tp = omm([(ps[2 + z][:, 0:256], WG[z][:, c, :], HO[:, c, :], c == 0, c == 7) for c in range(8)],
                             tl, t_od, tb)
                t_wfree = tp
                ta = oop("act", lambda e: e.activation(OS, ps[2][:, 0:256], ACT.Silu), tp, t_od)
                t_od = oop("dve", lambda e: e.tensor_tensor(OS, OS, ps[3][:, 0:256], M), ta)
                t_od = oop("dve", lambda e, j=j: e.tensor_tensor(OH[:, j, :], OS, ps[1][:, 0:256], M), t_od)
            t_hd = t_od
            for j in range(8):
                src = dr["moe"][index[("d", x)] - 8].rearrange("p (f n) -> p f n", f=4)[:, :, j * 128:j * 128 + 128]
                tl = oload(WD, src, *([t_dfree] if t_dfree else []))
                tp = omm([(ps[4][:, 0:256], WD[:, f, :], OH[:, f, :], f == 0, f == 3) for f in range(4)], tl, t_od)
                t_dfree = tp
                t_od = oop("dve", lambda e, j=j: e.tensor_tensor(XT[:, j, :], XT[:, j, :], ps[4][:, 0:256], ADD), tp)

        def guard(eng):
            wait(eng, fence + [t_flag])

            def emit(e, eng=eng):
                v = e.value_load(flag[0:1, 0:1], min_val=0, max_val=1)
                with e.If(v > 0):
                    for f in over[eng]:
                        f(e)
                    e.wait_ge(*t_od)
            queue[eng].append(emit)

        t_moe = [t_acc[q] for q in range(4)]
        for eng in ("pe", "dve", "act", "pool"):
            guard(eng)

        XG = A(4096, 8, 256)
        SQ = A(6144, 8, 256)
        RB = A(o + 512, 4, 256)
        XN = A(2048, 8, 256)
        TM = A(o + 1536, 4, 256)
        t_xg = scale_cols(XG, XT, "g_ple", *t_moe)
        t_sq = squares(SQ, XT, [t_moe[c // 2] for c in range(8)])
        w, t_w = slot(("pgate", 0))
        t_p = []
        t_xn, t_g3, t_sq1, t_sq2 = [], [], [], []
        XN2 = A(8192, 8, 256)
        banks = [0, 1, 2, 3, 4, 5, 6]
        def ple_out(j):
            b, tok = t_p[j]
            k = j % 4
            a = tt(TM[:, k, :], ps[b][:, 0:256], RB[:, 0, :], M, tok, t_r3, *([t_xn[j - 4]] if j >= 4 else []))
            bank_free[b] = [a]
            a = act(TM[:, k, :], TM[:, k, :], ACT.Sigmoid, a)
            a = tt(TM[:, k, :], TM[:, k, :], PP[:, j, :], M, a, t_pp[j])
            a = tt(XT[:, j, :], XT[:, j, :], TM[:, k, :], ADD, a)
            t_xn.append(a)
            g = ts(XN[:, j, :], XT[:, j, :], vcol("g_final", j), None, M, None, a)
            t_g3.append(g)
            t_sq1.append(act(SQ[:, j, :], XT[:, j, :], ACT.Square, a, t_m))
            t_sq2.append(act(XN2[:, j, :], XN[:, j, :], ACT.Square, g))

        for j in range(8):
            if j == 1:
                t_m = mean_pe(7, 0, SQ, inv1024, t_sq)
                t_r3 = rsqrt(RB[:, 0, :], ps[7][:, 0:256], t_m)
                bank_free[7] = [t_r3]
            w, t_w = slot(("pgate", j // 4))
            w = w.rearrange("p (c n) -> p c n", c=8)
            b = banks[j % 7]
            wait("pe", bank_free[b])
            for c in range(8):
                tok = mms([(ps[b][:, 0:256], w[:, c, (j % 4) * 128:(j % 4) * 128 + 128], XG[:, c, :], c == 0, c == 7)],
                          t_w, t_xg[c])
            if j % 4 == 3:
                free(("pgate", j // 4), tok)
            t_p.append((b, tok))
            if j >= 1:
                ple_out(j - 1)
        ple_out(7)

        t_m1 = mean_pe(7, 0, SQ, inv1024, t_sq1)
        t_r4 = rsqrt(RB[:, 1, :], ps[7][:, 0:256], t_m1)
        bank_free[7] = [t_r4]
        t_m2 = mean_pe(6, 0, XN2, inv1024, t_sq2)
        a = tt(RB[:, 2, :], RB[:, 1, :], RB[:, 1, :], M, t_r4)
        a = tt(RB[:, 2, :], RB[:, 2, :], ps[6][:, 0:256], M, a, t_m2)
        bank_free[6] = [a]
        a = rsqrt(RB[:, 2, :], RB[:, 2, :], a)
        t_r45 = tt(RB[:, 2, :], RB[:, 2, :], RB[:, 1, :], M, a)
        H5 = A(6144, 8, 256)
        t_h5 = [stt(H5[:, c, :], XN[:, c, :], vcol("pre2", c), RB[:, 2, :], M, M, t_r45, t_m1, t_g3[c]) for c in range(8)]
        t_x4 = [tt(XT[:, c, :], XN[:, c, :], RB[:, 1, :], M, t_r4) for c in range(8)]
        SGC = A(2048, 8, 256)
        SGA = A(4096, 8, 256)
        CU = A(10240, 4, 286)
        CA = A(8192, 4, 256)
        QT = A(8192 + 1024, 4, 256)
        KT = A(o + 2560, 4, 256)
        VT = A(o + 3584, 2, 512)
        ZM = A(11384, 2, 384)
        o2 = o + 4608
        AB = A(o2, 2, 384)
        AT = A(o2 + 768, 4, 256)
        assert 11384 + 768 <= o

        GS = KT
        t_gs = []

        def ev_gs(j, p, tok):
            t_gs.append(act(GS[:, j, :], p, ACT.Sigmoid, tok))
            return [t_gs[-1]]

        free(("in2", 0), project(("in2", 0), 4, H5, t_h5, ev_gs, [0, 1, 2, 3]))
        t_cpad = op("dve", lambda e: e.memset(CU[:, :, 0:30], 0.0))
        t_glu = []

        def ev_glu(j, p, tok):
            t_glu.append(tt(CU[:, j, 30:286], p, GS[:, j, :], M, tok, t_gs[j]))
            return [t_glu[-1]]

        free(("in2", 1), project(("in2", 1), 4, H5, t_h5, ev_glu, [4, 5, 6, 7]))
        taps = []
        t_tap = {}

        def tap(j, k):
            src = CU[:, j, k:k + 256]
            wv = vec[:, VEC["dw_w"] + 4 * k + j:VEC["dw_w"] + 4 * k + j + 1]
            if k == 0:
                t_tap[j] = ts(CA[:, j, :], src, wv, vcol("dw_b", j), M, ADD, t_glu[j], t_cpad, t_m2)
            else:
                t_tap[j] = stt(CA[:, j, :], src, wv, CA[:, j, :], M, ADD, t_tap[j])

        for k in range(31):
            for j in range(4):
                taps.append((j, k))

        def some_taps(n):
            for _ in range(min(n, len(taps))):
                tap(*taps.pop(0))

        t_q, t_k, t_vv = [], [], []

        def ev_q(j, p, tok):
            t_q.append(act(QT[:, j, :], p, ACT.Copy, tok, t_m2))
            return [t_q[-1]]

        def ev_k(j, p, tok):
            t_k.append(act(KT[:, j, :], p, ACT.Copy, tok, t_glu[3]))
            return [t_k[-1]]

        free(("in2", 2), project(("in2", 2), 4, H5, t_h5, ev_q, [0, 1, 2, 3]))
        some_taps(32)
        free(("in2", 3), project(("in2", 3), 4, H5, t_h5, ev_k, [4, 5, 6, 7]))
        w, t_w = slot(("in2", 4))
        w = w.rearrange("p (c n) -> p c n", c=8)
        for i in range(2):
            lst = [(ps[i][:, :], H5[:, c, i * 128:i * 128 + 128], w[:, c, :], c == 0, c == 7) for c in range(8)]
            tok = mms(lst, t_w, *bank_free[i])
            t_vv.append(act(VT[:, i, :], ps[i][:, :], ACT.Copy, tok))
            bank_free[i] = [t_vv[i]]
        free(("in2", 4), tok)
        some_taps(16)
        t_att, t_zm, t_av = {}, {}, {}
        t_c2 = {}

        def scores(h):
            b = 2 + h % 2
            r = 64 * (h % 2)
            j = h // 2
            tok = mms([(ps[b][:, 0:256], KT[r:r + 64, j, 0:128], QT[r:r + 64, j, :], True, True),
                       (ps[b][:, 256:384], KT[r:r + 64, j, 128:256], QT[r:r + 64, j, 128:256], True, True)],
                      t_q[j], t_k[j], *bank_free[b])
            k = h % 2
            old = [t_c2[h - 2]] if h >= 2 else []
            t_zm[h] = stt(ZM[:, k, :], ps[b][:, 0:384], 0.125, nm, M, ADD, tok, *old)
            bank_free[b] = [t_zm[h]]
            old = [t_av[h - 2]] if h >= 2 else []
            x = AB[:, k, :]
            a = act(x, ZM[:, k, :], ACT.Abs, t_zm[h], *old)
            a = act(x, x, ACT.Exp, a, scale=-1.0)
            a = act(x, x, ACT.Ln, a, bias=1.0)
            return stt(x, ZM[:, k, :], 0.0, x, MAX, ADD, a)

        def suffix(h, t_p):
            b = 4 + h % 2
            k = h % 2
            x = AB[:, k, :]
            tok = mms([(ps[b][:, 0:256], tri, x[:, 0:256], True, False),
                       (ps[b][:, 128:256], one, x[:, 256:384], False, True),
                       (ps[b][:, 256:384], tri, x[:, 256:384], True, True)], t_p, *bank_free[b])
            a = tt(x, ZM[:, k, :], ps[b][:, 0:384], SUB, tok)
            t_c2[h] = a
            bank_free[b] = [a]
            return act(x, x, ACT.Exp, a)

        t_attT = [None] * 4

        def values(h, t_a):
            b = 6 + (h // 2) % 2
            r = 64 * (h % 2)
            x = AB[:, h % 2, :]
            tok = mms([(ps[b][r:r + 64, 0:256], VT[:, 0, h * 64:h * 64 + 64], x[:, 0:256], True, False),
                       (ps[b][r:r + 64, 128:256], VT[:, 1, h * 64:h * 64 + 64], x[:, 256:384], False, True)],
                      t_a, *t_vv, *(bank_free[b] if h % 2 == 0 else []))
            t_av[h] = tok
            if h % 2:
                j = h // 2
                t_attT[j] = act(AT[:, j, :], ps[b][:, 0:256], ACT.Copy, tok)
                bank_free[b] = [t_attT[j]]


        p, a_ = {}, {}
        G0 = [("in2", 5), ("in2", 6), ("in2", 7), ("in2", 8)]
        t_sg = {}

        def gates(n, half):
            key = G0[n]
            w, t_w = slot(key)
            w = w.rearrange("p (c n) -> p c n", c=8)
            dst = SGC if n < 2 else SGA
            for j in (2 * half, 2 * half + 1):
                b = j % 2
                tok = mms([(ps[b][:, 0:256], w[:, c, j * 128:j * 128 + 128], H5[:, c, :], c == 0, c == 7)
                           for c in range(8)], t_w, *bank_free[b])
                jj = 4 * (n % 2) + j
                t_sg[n // 2, jj] = act(dst[:, jj, :], ps[b][:, 0:256], ACT.Sigmoid, tok, t_x4[7], t_h5[7])
                bank_free[b] = [t_sg[n // 2, jj]]
            if half:
                free(key, tok)

        for s in range(10):
            if s < 8:
                p[s] = scores(s)
            if 1 <= s <= 8:
                a_[s - 1] = suffix(s - 1, p[s - 1])
            if s < 8:
                gates(s // 2, s % 2)
            if 1 <= s <= 8:
                values(s - 1, a_[s - 1])
            some_taps(10)
        some_taps(1000)

        fence = all_last()
        TMP = A(6144, 4, 256)
        MU = A(6144 + 1024, 256)
        RS = A(6144 + 1280, 256)
        t_m = mean_pe(0, 0, CA, inv512, [t_tap[j] for j in range(4)])
        t_xc = []
        for j in range(4):
            t_xc.append(tt(CA[:, j, :], CA[:, j, :], ps[0][:, 0:256], SUB, t_m))
        bank_free[0] = [t_xc[3]]
        wait("act", fence)
        wait("dve", fence)
        t_s = [act(TMP[:, j, :], CA[:, j, :], ACT.Square, t_xc[j]) for j in range(4)]
        t_m = mean_pe(1, 0, TMP, inv512, t_s)
        t_rs = rsqrt(RS, ps[1][:, 0:256], t_m)
        bank_free[1] = [t_rs]
        t_cs = []
        for j in range(4):
            a = tt(CA[:, j, :], CA[:, j, :], RS, M, t_rs)
            t_cs.append(act(CA[:, j, :], CA[:, j, :], ACT.Silu, a, scale=vcol("ln_g", j), bias=vcol("ln_b", j)))
        MG = A(10240, 8, 256)
        wc, t_wc = slot(("cb", 0))
        wc = wc.rearrange("p (c n) -> p c n", c=4)
        wa, t_wa = slot(("ab", 0))
        wa = wa.rearrange("p (c n) -> p c n", c=4)
        t_ma = []
        for j in range(8):
            b = 2 + j % 3
            tok = mms([(ps[b][:, 0:256], wa[:, c, j * 128:j * 128 + 128], AT[:, c, :], c == 0, c == 3)
                       for c in range(4)], t_wa, *t_attT, *bank_free[b])
            a = tt(SGA[:, j, :], SGA[:, j, :], ps[b][:, 0:256], M, tok, t_sg[1, j])
            bank_free[b] = [a]
            t_ma.append(a)
        free(("ab", 0), tok)
        t_mg = []
        for j in range(8):
            b = 5 + j % 3
            tok = mms([(ps[b][:, 0:256], wc[:, c, j * 128:j * 128 + 128], CA[:, c, :], c == 0, c == 3)
                       for c in range(4)], t_wc, *t_cs, *bank_free[b])
            a = stt(SGC[:, j, :], ps[b][:, 0:256], vcol("b_cb", j), SGC[:, j, :], ADD, M, tok, t_sg[0, j])
            bank_free[b] = [a]
            t_mg.append(tt(MG[:, j, :], SGC[:, j, :], SGA[:, j, :], ADD, a, t_ma[j]))
        free(("cb", 0), tok)
        MX = A(2048, 8, 256)
        SQ = A(4096, 8, 256)
        fence = all_last()
        wait("act", fence)
        t_mx, t_sq = [], []

        for n in range(2):
            def ev(j, p, tok, n=n):
                jj = 4 * n + j
                t_sq.append(act(SQ[:, jj, :], p, ACT.Square, tok))
                t_mx.append(act(MX[:, jj, :], p, ACT.Copy, tok, t_vec, scale=vcol("post2", jj)))
                return [t_mx[-1]]
            free(("out2", n), project(("out2", n), 4, MG, t_mg, ev, [0, 1, 2, 3]))
        t_m = mean_pe(4, 0, SQ, inv1024, t_sq)
        R6 = A(o + 512, 256)
        R7 = A(o + 768, 256)
        t_r6 = rsqrt(R6, ps[4][:, 0:256], t_m)
        bank_free[4] = [t_r6]
        XG = A(6144, 8, 256)
        t_x5, t_xg, t_sq = [], [], []
        for j in range(8):
            a = tt(MX[:, j, :], MX[:, j, :], R6, M, t_r6, t_mx[j])
            a = tt(XT[:, j, :], XT[:, j, :], MX[:, j, :], ADD, a)
            t_x5.append(a)
            t_xg.append(act(XG[:, j, :], XT[:, j, :], ACT.Copy, a, scale=vcol("fpre2", j)))
            t_sq.append(act(SQ[:, j, :], XT[:, j, :], ACT.Square, a, t_m))
        H7 = A(2048, 8, 256)
        FF = A(8192, 22, 256)
        TG = A(13824, 4, 256)
        R7 = A(14848, 256)
        GB = A(15104, 1024)
        SM2 = A(16128, 8)
        fence = all_last()
        wait("act", fence)
        t_gb = load("act", GB, dr["gpost"].partition_broadcast(128), sem("l_gb"))
        fb = [0, 1, 2, 3, 4, 5, 6]
        ix = [0]
        t_ff = []
        t_r7 = None
        t_tg = {}
        for s in range(11):
            w, t_w = slot(("fup", s))
            w = w.rearrange("p (c n) -> p c n", c=8)
            src, t_src = (XG, t_xg) if s == 0 else (H7, t_h7)
            pend = []
            for j in range(2):
                bs = []
                for z in range(2):
                    b = fb[ix[0] % 7]
                    ix[0] += 1
                    wait("pe", bank_free[b])
                    for c in range(8):
                        at = z * 256 + j * 128
                        tok = mms([(ps[b][:, 0:256], w[:, c, at:at + 128], src[:, c, :], c == 0, c == 7)], t_w,
                                  t_src[c])
                    bs.append((b, tok))
                pend.append((2 * s + j, bs))
                if s == 0 and j == 0:
                    t_m = mean_pe(7, 0, SQ, inv1024, t_sq)
                    t_r7 = rsqrt(R7, ps[7][:, 0:256], t_m, *fence)
                    bank_free[7] = [t_r7]
                    t_h7 = [tt(H7[:, c, :], XG[:, c, :], R7, M, t_r7, t_xg[c]) for c in range(8)]
            free(("fup", s), tok)
            for jj, ((b0, k0), (b1, k1)) in pend:
                g = TG[:, jj % 2, :]
                u = TG[:, 2 + jj % 2, :]
                old = [t_ff[jj - 2]] if jj >= 2 else []
                if s == 0:
                    a = tt(g, ps[b0][:, 0:256], R7, M, k0, t_r7, *old)
                    bank_free[b0] = [a]
                    a = act(g, g, ACT.Silu, a)
                    bb = tt(u, ps[b1][:, 0:256], R7, M, k1, t_r7)
                    bank_free[b1] = [bb]
                    t_ff.append(tt(FF[:, jj, :], g, u, M, a, bb, *fence))
                else:
                    a = act(g, ps[b0][:, 0:256], ACT.Silu, k0, *old)
                    bank_free[b0] = [a]
                    t_ff.append(tt(FF[:, jj, :], ps[b1][:, 0:256], g, M, a, k1))
                    bank_free[b1] = [t_ff[-1]]
            if s == 4:
                X5 = A(4096, 2, 1024)
                t_x5k = []
                for i in range(2):
                    for q in range(2):
                        b = fb[ix[0] % 7]
                        ix[0] += 1
                        tok = tts([(ps[b][:, c * 128:c * 128 + 128], XT[:, 4 * q + c, i * 128:i * 128 + 128])
                                   for c in range(4)], ident, *t_x5, *bank_free[b])
                        k = act(X5[:, i, q * 512:q * 512 + 512], ps[b][:, :], ACT.Copy, tok, t_m)
                        bank_free[b] = [k]
                        t_x5k.append(k)
        s_out = sem("s_out")
        OUT = XG
        OUT = A(6144, 2, 1024)
        SCR = A(2048, 2, 1024)
        t_lastup = tok
        for i in range(2):
            ss = SM2[:, 2 * i:2 * i + 2]
            t = []
            for n in range(2):
                wait("pe", bank_free[2 * i + n])
            for k in range(22):
                w, t_w = slot(("fdn", k // 4))
                w = w.rearrange("p (c n) -> p c n", c=4)
                for n in range(2):
                    tok = mms([(ps[2 * i + n][:, :], FF[:, k, i * 128:i * 128 + 128],
                                w[:, k % 4, n * 512:n * 512 + 512], k == 0, k == 21)], t_w, t_ff[k])
                if i == 1 and k % 4 == 3 or k == 21:
                    free(("fdn", k // 4), tok)
            for n in range(2):
                t.append(act(SCR[:, i, n * 512:n * 512 + 512], ps[2 * i + n][:, :], ACT.Square, tok, t_lastup,
                             scale=1.0 / 32, accum_out=ss[:, n:n + 1]))
            rr = SM2[:, 4 + i:5 + i]
            a = tt(rr, ss[:, 0:1], ss[:, 1:2], ADD, *t)
            a = rsqrt(rr, rr, a)
            for n in range(2):
                sl = slice(n * 512, n * 512 + 512)
                k = stt(OUT[:, i, sl], ps[2 * i + n][:, :], rr, GB[:, sl], M, M, a, t_gb, t_lastup)
                k = tt(OUT[:, i, sl], OUT[:, i, sl], X5[:, i, sl], ADD, k, *t_x5k)
                load("act", out_ap[0, i * 128:i * 128 + 128, sl], OUT[:, i, sl], s_out, k)
        wait("act", [(s_out, 64)])

        src_of = {"in1": "w_in", "out1": "w_out", "pproj": "w_pp", "pgate": "w_pg", "in2": "w_in2", "cb": "w_cb",
                  "ab": "w_ab", "out2": "w_out2", "fup": "w_up2", "fdn": "w_dn2"}
        for i, (name, n) in enumerate(order):
            src = dr["moe"][i - 8] if name in "gud" else dr[src_of[name]][n]
            if (name, n) == ("fdn", 5):
                src = src[:, 0:2048]
            dst = ring[:, i % RING, 0:src.shape[1]]
            wait("sp", [freed[i - RING]] if i >= RING else [])
            queue["sp"].append(lambda e, dst=dst, src=src, i=i: e.dma_start(dst, src).then_inc(ring_sem[i % RING], 16))

        block = ctx.enter_context(nc.Block())

        @block.tensor
        def _(e):
            for f in queue["pe"]:
                f(e)

        @block.vector
        def _(e):
            for f in queue["dve"]:
                f(e)

        @block.scalar
        def _(e):
            for f in queue["act"]:
                f(e)

        @block.gpsimd
        def _(e):
            for f in queue["pool"]:
                f(e)

        @block.sync
        def _(e):
            for f in queue["sp"]:
                f(e)


def _cols(a, n):
    k = a.shape[0]
    w = a.shape[1] // n
    return np.ascontiguousarray(a.reshape(k // 128, 128, n, w).transpose(2, 1, 0, 3)).reshape(n, 128, -1)


def _feat(v):
    return v.reshape(-1, 128).T


def _layout(i):
    r = {}
    x = i["x"][0]
    r["x"] = np.ascontiguousarray(x.reshape(2, 128, 1024).transpose(1, 0, 2))
    r["xT"] = np.ascontiguousarray(x.T.reshape(8, 128, 256).transpose(1, 0, 2))
    r["pT"] = np.ascontiguousarray(i["p"][0, 0].T.reshape(2, 128, 256).transpose(1, 0, 2))
    w = i["w_in"][0]
    r["w_in"] = _cols(np.concatenate([w[:, 2048:], w[:, 1536:2048], w[:, 512:1024], w[:, 1024:1536], w[:, :512]], 1), 5)
    r["w_out"] = _cols(i["w_out"][0], 2)
    pp = i["w_ple_proj"][0]
    r["w_pp"] = _cols(pp, 1)
    r["w_pg"] = _cols(i["w_ple_gate"][0], 2)
    g, u, d = (i[k][0].reshape((NE,) + i[k].shape[3:]) for k in ("w_gate", "w_up", "w_down"))
    src = {"g": g, "u": u, "d": d}
    moe = np.empty((96, 128, SLOT), g.dtype)
    for n, (k, e) in enumerate(moe_order()):
        moe[n] = _cols(src[k][e], 1)[0]
    r["moe"] = moe
    w = i["w_in_2"]
    r["w_in2"] = _cols(np.concatenate([w[:, 512:1024], w[:, 0:512], w[:, 1024:]], 1), 9)
    r["w_cb"] = _cols(i["w_conv_branch_2"], 1)
    r["w_ab"] = _cols(i["w_att_branch_2"], 1)
    r["w_out2"] = _cols(i["w_out_2"], 2)
    w = i["w_ffn_up_2"].reshape(1024, 2, 11, 256).transpose(0, 2, 1, 3).reshape(1024, 5632)
    r["w_up2"] = _cols(w, 11)
    dn = i["w_ffn_down_2"]
    dn = np.concatenate([dn, dn[:256]], 0)
    r["w_dn2"] = np.ascontiguousarray(dn.reshape(6, 4, 128, 1024).transpose(0, 2, 1, 3)).reshape(6, 128, SLOT)
    wr = np.concatenate([i["w_group"][0], i["w_router"][0].transpose(1, 0, 2).reshape(1024, 32)], 1)
    r["wr"] = np.ascontiguousarray(wr.reshape(8, 128, 36).transpose(1, 0, 2))
    r["lbias"] = np.concatenate([i["b_group"][0], i["b_router"][0].reshape(-1)])[None]
    r["wsT"] = np.ascontiguousarray(i["w_spatial"][0].transpose(2, 0, 1)).reshape(128, 1024)
    r["b_sp"] = np.ascontiguousarray(i["b_spatial"][0].reshape(4, 2, 128).transpose(1, 0, 2))
    r["gpost"] = i["norm_ffn_post_2"][None]
    v = [_feat(i["g_mix"][0]), i["w_conv"][0].reshape(12, 128).T, _feat(i["g_sgu"][0]), _feat(i["g_ffn"][0]),
         _feat(i["g_ple"][0]), _feat(i["g_final"]), _feat(i["norm_mix_pre_2"]),
         i["conv_dw_w_2"].reshape(124, 128).T, _feat(i["conv_dw_b_2"]), _feat(i["conv_ln_g_2"]),
         _feat(i["conv_ln_b_2"]), _feat(i["b_conv_branch_2"]), _feat(i["norm_mix_post_2"]),
         _feat(i["norm_ffn_pre_2"])]
    r["vec"] = np.ascontiguousarray(np.concatenate(v, 1))
    c = np.zeros((128, N_CST), np.float32)
    k = np.arange(128)
    c[:, C_ID:C_ID + 128] = np.eye(128)
    c[:, C_U:C_U + 128] = k[:, None] < k[None]
    c[:, C_TRI:C_TRI + 128] = k[:, None] >= k[None]
    nmd = np.where(k[:, None] < k[None], 0.0, -1e30)
    c[:, C_NM:C_NM + 128] = nmd
    c[:, C_NM + 256:C_NM + 384] = nmd
    c[:, C_IOTA:C_IOTA + CAP] = np.arange(CAP)
    c[:, C_IX:C_IX + 8] = np.arange(8) - 64.0
    r["cst"] = c
    return r


def kernel(**inputs):
    import concourse.bacc as bacc
    from concourse.bass_utils import run_bass_kernel_spmd

    nc = bacc.Bacc("TRN2", target_bir_lowering=False, num_devices=1)
    arrays, dr = {}, {}
    for name, a in _layout({k: np.asarray(v) for k, v in inputs.items()}).items():
        a = np.ascontiguousarray(a)
        arrays["in_" + name] = a
        dr[name] = nc.dram_tensor("in_" + name, a.shape, mybir.dt.from_np(a.dtype), kind="ExternalInput").ap()
    out = nc.dram_tensor("out_0", (1, T, D), F32, kind="ExternalOutput").ap()
    build(nc, dr, out)
    r = run_bass_kernel_spmd(nc, [arrays], core_ids=[0])
    return r.results[0]["out_0"]
```

```python
from contextlib import ExitStack

import numpy as np

import concourse.bass as bass
from concourse import mybir

F32 = mybir.dt.float32
R32 = mybir.dt.float32r
I32 = mybir.dt.int32
ALU = mybir.AluOpType
ACT = mybir.ActivationFunctionType
AX = mybir.AxisListType.X

T = 256
D = 1024
NE = 32
CAP = 64
NP = NE // 2
EPS = 1e-6
RING = 8
N0 = 7
N1 = N0 + 97
SLOTS = ([0, 1, 2, 3, 8, 0, 1], [2, 3, 8, 0, 1, 9, 5, 7, 4, 6], [2, 3, 0, 1])
SLOT = 4096

C_ID, C_U, C_TRI, C_NM, C_IOTA, C_IX = 0, 128, 256, 384, 768, 832
N_CST = 840
VEC = {}
_at = 0
for _n, _w in (("g_mix", 8), ("w_conv", 12), ("g_sgu", 4), ("g_ffn", 8), ("g_ple", 8), ("g_final", 8),
               ("pre2", 8), ("dw_w", 124), ("dw_b", 4), ("ln_g", 4), ("ln_b", 4), ("b_cb", 8), ("post2", 8),
               ("fpre2", 8)):
    VEC[_n] = _at
    _at += _w
N_VEC = _at


def moe_order():
    return [(k, 2 * q + r) for q in range(NP) for k in "gud" for r in range(2)]


def stream():
    out = [("in1", i) for i in range(5)] + [("out1", i) for i in range(2)]
    m = moe_order()
    out += m[:12] + [("pproj", 0)] + m[12:]
    out += [("pgate", i) for i in range(2)] + [("in2", i) for i in range(9)]
    out += [("ab", 0), ("cb", 0)] + [("out2", i) for i in range(2)]
    out += [("fup", i) for i in range(11)] + [("fdn", i) for i in range(6)]
    return out


def build(nc, dr, out_ap):
    ctx = ExitStack()
    with ctx:
        def sem(name):
            return ctx.enter_context(nc.semaphore(name))

        ring = ctx.enter_context(nc.sbuf_tensor("ring", [128, RING, SLOT], F32))
        ring_at = nc.sbuf_base - 4 * RING * SLOT
        cst = ctx.enter_context(nc.sbuf_tensor("cst", [128, N_CST], F32))
        vec = ctx.enter_context(nc.sbuf_tensor("vec", [128, N_VEC], F32))
        wr = ctx.enter_context(nc.sbuf_tensor("wr", [128, 8, 36], F32))
        ones = ctx.enter_context(nc.sbuf_tensor("ones", [128, 3, 128], F32))
        flag = ctx.enter_context(nc.sbuf_tensor("flag", [128, 1], I32))
        eps = ctx.enter_context(nc.sbuf_tensor("eps", [128, 1], F32))
        NAR = 22528
        arena = ctx.enter_context(nc.sbuf_tensor("arena", [128, NAR], F32))
        arena_at = nc.sbuf_base - 4 * NAR
        ps = [ctx.enter_context(nc.psum_tensor(f"ps{i}", [128, 512], F32)) for i in range(8)]

        def A(at, *shape):
            n = 1
            for s in shape:
                n *= s
            assert at + n <= NAR, (at, n)
            v = arena[:, at:at + n]
            if len(shape) == 2:
                v = v.rearrange("p (a b) -> p a b", a=shape[0])
            elif len(shape) == 3:
                v = v.rearrange("p (a b c) -> p a b c", a=shape[0], b=shape[1])
            return v

        def rounded(name, at, *shape):
            return nc.alloc_sbuf_tensor_at(name, [128, *shape], R32, offset=arena_at + 4 * at)

        names = ("pe", "dve", "act", "pool", "sp")
        queue = {n: [] for n in names}
        done_sem = {n: sem("done_" + n) for n in names}
        count = {n: 0 for n in names}
        seen = {n: {} for n in names}

        def wait(eng, toks):
            for tok in toks:
                s, v = tok
                if seen[eng].get(id(s), 0) < v:
                    seen[eng][id(s)] = v
                    queue[eng].append(lambda e, s=s, v=v: e.wait_ge(s, v))

        def op(eng, fn, *toks):
            wait(eng, toks)
            count[eng] += 1
            s = done_sem[eng]
            queue[eng].append(lambda e: fn(e).then_inc(s, 1))
            return (s, count[eng])

        def last(eng):
            return (done_sem[eng], count[eng])

        def all_last():
            return [last(n) for n in ("pe", "dve", "act") if count[n]]

        def load(eng, dst, src, s, *toks):
            wait(eng, toks)
            queue[eng].append(lambda e: e.dma_start(dst, src).then_inc(s, 16))
            return (s, 16)

        def mms(lst, *toks):
            wait("pe", toks)
            for o, l, r, a, z in lst[:-1]:
                queue["pe"].append(lambda e, o=o, l=l, r=r, a=a, z=z: e.matmul(
                    o, l, r, start=a, stop=z, skip_group_check=True))
            o, l, r, a, z = lst[-1]
            return op("pe", lambda e: e.matmul(o, l, r, start=a, stop=z, skip_group_check=True))

        def tts(lst, ident, *toks):
            wait("pe", toks)
            for o, i in lst[:-1]:
                queue["pe"].append(lambda e, o=o, i=i: e.transpose(o, i, ident))
            o, i = lst[-1]
            return op("pe", lambda e: e.transpose(o, i, ident))

        bank_free = [[] for _ in range(8)]

        def tt(o, a, b, f, *toks, eng="dve"):
            return op(eng, lambda e: e.tensor_tensor(o, a, b, f), *toks)

        def ts(o, a, s1, s2, f0, f1, *toks, eng="dve"):
            if f1 is None:
                return op(eng, lambda e: e.tensor_scalar(o, a, s1, s2, f0), *toks)
            return op(eng, lambda e: e.tensor_scalar(o, a, s1, s2, f0, f1), *toks)

        def stt(o, a, s, b, f0, f1, *toks):
            return op("dve", lambda e: e.scalar_tensor_tensor(out=o, in0=a, scalar=s, in1=b, op0=f0, op1=f1), *toks)

        def act(o, a, f, *toks, **kw):
            return op("act", lambda e: e.activation(o, a, f, **kw), *toks)

        def tables(name):
            queue["act"].append(lambda e: e.preload_act_table_set(name))

        def red(o, a, f, *toks):
            return op("dve", lambda e: e.tensor_reduce(o, a, AX, f), *toks)

        M, ADD, SUB, MAX = ALU.mult, ALU.add, ALU.subtract, ALU.max

        order = stream()
        index = {k: i for i, k in enumerate(order)}
        moe_at = {k: i for i, k in enumerate(moe_order())}
        ring_sem = [sem(f"ring{i}") for i in range(10)]
        s_half = sem("half")
        freed = {}

        place, fills = [], [0] * 10
        for i in range(len(order)):
            k = SLOTS[0][i] if i < N0 else SLOTS[1][(i - N0) % 10] if i < N1 else SLOTS[2][(i - N1) % 4]
            if i == N1 - 1:
                k = 4
            fills[k] += 1
            place.append((k, fills[k]))

        def view(k):
            return ring[:, k, :] if k < 8 else A((18432, 10240)[k - 8], SLOT)

        def slot(key):
            k, n = place[index[key]]
            return view(k), (ring_sem[k], 16 * n)

        def free(key, *toks):
            freed[index[key]] = list(toks)

        ident = cst[:, C_ID:C_ID + 128]
        U = cst[:, C_U:C_U + 128]
        tri = cst[:, C_TRI:C_TRI + 128]
        nm = cst[:, C_NM:C_NM + 384]
        iota = cst[:, C_IOTA:C_IOTA + CAP]
        ix8 = cst[:, C_IX:C_IX + 8]
        one, inv1024, inv512 = ones[:, 0, :], ones[:, 1, :], ones[:, 2, :]

        def vcol(name, i):
            return vec[:, VEC[name] + i:VEC[name] + i + 1]

        WH = nc.alloc_sbuf_tensor_at("wh", [128, 8, 1024], R32, offset=ring_at + 16 * SLOT)
        WL = nc.alloc_sbuf_tensor_at("wl", [128, 8, 1024], R32, offset=ring_at + 24 * SLOT)
        pieces = []
        for key in order[:N0] + order[N1:]:
            name, n = key
            for j in range(2 if key == ("fdn", 5) else 4):
                pieces.append((key, j))
        n_piece = {k: i for i, k in enumerate(pieces)}
        t_hi, t_lo, piece_free = {}, {}, {}
        emitted = [0]

        def piece_view(v, key):
            if key[0] == "fdn":
                return v
            return v.rearrange("p (c n) -> p c n", c=4 if key[0] in ("cb", "ab") else 8)

        def split(i):
            key, j = pieces[i]
            k = i % 8
            w_, t_w = slot(key)
            if key == ("in1", 0) and j > 1:
                t_w = (s_half, 16)
            if key[0] == "fdn":
                src = w_[:, j * 1024:j * 1024 + 1024]
            elif key[0] in ("cb", "ab"):
                src = w_.rearrange("p (c n) -> p c n", c=4)[:, :, j * 256:j * 256 + 256]
            else:
                src = w_.rearrange("p (c n) -> p c n", c=8)[:, :, j * 128:j * 128 + 128]
            if i < 8:
                old = []
            elif 4 * N0 <= i < 4 * N0 + 8:
                old = [t for n in ((4, 6) if i % 8 < 4 else (5, 7)) for t in freed[max(x for x in range(N1) if place[x][0] == n)]]
            else:
                old = [piece_free[i - 8]]
            t_hi[i] = act(piece_view(WH[:, k, :], key), src, ACT.Copy, t_w, *old)
            eng = "dve" if i % 4 == 3 and not 4 * N0 - 8 <= i < 4 * N0 or i < 4 * N0 - 8 and i % 2 == 0 else "pool"
            t_lo[i] = tt(piece_view(WL[:, k, :], key), src, piece_view(WH[:, k, :], key), SUB, t_hi[i], *old,
                         eng=eng)
            if key not in n_split:
                n_split[key] = {}
            n_split[key][eng] = t_lo[i]
            freed[index[key]] = list(n_split[key].values())

        n_split = {}

        def ensure(n):
            while emitted[0] < min(n, len(pieces)):
                split(emitted[0])
                emitted[0] += 1

        def pair_of(dst_hi, dst_lo, src, *toks, eng="dve"):
            a = act(dst_hi, src, ACT.Copy, *toks)
            return tt(dst_lo, src, dst_hi, SUB, a, eng=eng)

        def three(out, key, j, hi, lo, t_src, cn=8, sub=0, last_use=True):
            i = n_piece[key, j]
            ensure(i + 1)
            wh = piece_view(WH[:, i % 8, :], key)
            wl = piece_view(WL[:, i % 8, :], key)
            wait("pe", [t_hi[i]])
            for c in range(cn):
                w_ = wh[:, c, sub * 128:sub * 128 + 128]
                mms([(out, w_, hi[:, c, :], c == 0, False), (out, w_, lo[:, c, :], False, False)], t_src[c])
            tok = mms([(out, wl[:, c, sub * 128:sub * 128 + 128], hi[:, c, :], False, c == cn - 1)
                       for c in range(cn)], t_lo[i])
            if last_use:
                piece_free[i] = tok
            return tok

        def wide(b, key, hi, lo, sl, t_src, last_use=False, order=(range(8),)):
            i0 = n_piece[key, 0]
            ensure(i0 + 4)
            k0 = i0 % 8
            assert k0 in (0, 4)
            wh, wl = (v[:, k0:k0 + 4, :].rearrange("p j (c n) -> p j c n", c=8) for v in (WH, WL))
            wait("pe", bank_free[b] + [t_hi[i0 + 3]])
            for half in order:
                for c in half:
                    mms([(ps[b][:, :], hi[:, c, sl], wh[:, :, c, :], c == order[0][0], False),
                         (ps[b][:, :], lo[:, c, sl], wh[:, :, c, :], False, False)], t_src[c])
                tok = mms([(ps[b][:, :], hi[:, c, sl], wl[:, :, c, :], False, c == order[-1][-1]) for c in half],
                          *[t_lo[i0 + x] for x in range(4)])
            if last_use:
                for x in range(4):
                    piece_free[i0 + x] = tok
            return tok

        def project3(key, hi, lo, t_src, evac, banks, ahead=6):
            for j in range(4):
                b = banks[j % len(banks)]
                wait("pe", bank_free[b])
                tok = three(ps[b][:, 0:256], key, j, hi, lo, t_src)
                bank_free[b] = evac(j, ps[b][:, 0:256], tok)
                ensure(n_piece[key, j] + 1 + ahead)
            return tok

        XT = A(0, 8, 256)
        XK = A(2048, 2, 1024)
        SQ0 = A(6144, 8, 256)
        PP = A(8192, 8, 256)
        SQ = A(10240, 8, 256)
        o = 12288
        VG = A(o, 2, 512)
        UG = A(o + 1024, 4, 256)
        Z = A(o + 2048, 4, 258)
        CR = A(o + 3080, 4, 256)
        BB = A(o + 4104, 4, 128)
        PT = A(o + 4864, 2, 256)
        SM = A(o + 5384, 720)
        WS = PP
        R2B = A(9216, 256)
        R1B = A(9472, 256)
        t_pp = []
        XGH, XGL = rounded("in_h", 10240, 8, 256), rounded("in_l", 0, 8, 256)
        MIXH, MIXL = rounded("mix_h", 6144, 8, 256), rounded("mix_l", 4096, 8, 256)

        t_xT = load("sp", XT, dr["xT"], sem("l_xT"))
        t_vec = load("sp", vec[:], dr["vec"], sem("l_vec"))
        first = len(queue["sp"])
        t_xk = load("sp", XK, dr["x"], sem("l_xk"))
        s_bb = sem("l_bb")
        t_ws = load("sp", WS[:, 0:4, :].rearrange("p a b -> p (a b)"), dr["wsT"], sem("l_ws"))
        load("sp", BB[0:64], dr["b_sp"][0:1, :, :].partition_broadcast(64), s_bb)
        load("sp", BB[64:128], dr["b_sp"][1:2, :, :].partition_broadcast(64), s_bb)
        t_bb = (s_bb, 32)
        t_cst = load("sp", cst[:], dr["cst"], sem("l_cst"))
        t_wr = load("sp", wr[:], dr["wr"], sem("l_wr"))
        t_pT = load("sp", PT, dr["pT"], sem("l_pT"))
        LB = SM[:, 0:36]
        t_lb = load("sp", LB, dr["lbias"].partition_broadcast(128), sem("l_lb"))
        late = queue["sp"][first:]
        del queue["sp"][first:]
        behind = {1: late[:1], 2: late[1:4], 3: late[4:]}

        tables("sqrt_and_others")
        t_eps = op("dve", lambda e: e.memset(eps[:], EPS))
        op("dve", lambda e: e.memset(ones[:, 0, :], 1.0))
        op("dve", lambda e: e.memset(ones[:, 1, :], 1.0 / 1024))
        t_ones = op("dve", lambda e: e.memset(ones[:, 2, :], 1.0 / 512))
        t_zpad = op("dve", lambda e: e.memset(Z[:, :, 0:2], 0.0))

        def squares(dst, src, toks):
            return [act(dst[:, c, :], src[:, c, :], ACT.Square, toks[c]) for c in range(len(toks))]

        def mean_pe(bank, at, src, w, toks):
            n = len(toks)
            wait("pe", bank_free[bank])
            for c in range(n):
                tok = mms([(ps[bank][:, at:at + 256], w, src[:, c, :], c == 0, c == n - 1)], toks[c])
            return tok

        def rsqrt(dst, src, *toks):
            a = act(dst, src, ACT.Sqrt, t_eps, *toks, bias=eps[:, 0:1])
            return op("dve", lambda e: e.reciprocal(dst, dst), a)

        t_xg, t_sq = [], []
        for c in range(8):
            a = act(XGH[:, c, :], XT[:, c, :], ACT.Copy, t_xT, t_vec, scale=vcol("g_mix", c))
            t_sq.append(tt(SQ0[:, c, :], XT[:, c, :], XT[:, c, :], M, t_xT, eng="pool" if c % 2 else "dve"))
            t_xg.append(stt(XGL[:, c, :], XT[:, c, :], vcol("g_mix", c), XGH[:, c, :], M, SUB, t_sq[c], a))

        t_u = []
        for j in range(4):
            b = 3 + j
            tok = three(ps[b][:, 0:256], ("in1", 0), j, XGH, XGL, t_xg)
            if j == 0:
                t_m = mean_pe(2, 0, SQ0, inv1024, t_sq)
                ensure(4)
                t_r1b = rsqrt(R1B, ps[2][:, 0:256], t_m)
                t_r2b = tt(R2B, R1B, R1B, M, t_r1b)
                bank_free[2] = [t_r1b]
            a = tt(UG[:, j, :], ps[b][:, 0:256], R1B, M, tok, t_r1b)
            bank_free[b] = [a]
            t_u.append(a)
            ensure(j + 6)
        RT = SM[:, 40:42]
        for i in range(2):
            t_rt = act(VG.rearrange("p a b -> p (a b)"), XK[:, i, :], ACT.Square, t_xk, last("act"), scale=1.0 / 32,
                       accum_out=RT[:, i:i + 1])
        t_rt = rsqrt(RT, RT, t_rt)
        t_u = [act(UG[:, j, :], UG[:, j, :], ACT.Gelu_apprx_tanh, t_u[j]) for j in range(4)]

        t_v = []
        for i in range(2):
            t_v.append(wide(i, ("in1", 1), XGH, XGL, slice(i * 128, i * 128 + 128), t_xg, i == 1))
        ensure(12)
        wsv = WS[:, 0:4, :].rearrange("p a (h t) -> p (a h) t", h=2)
        t_msk = op("pool", lambda e: e.affine_select(
            out=wsv, in_=wsv, compare_op=ALU.is_ge, fill=0.0, base=0, pattern=[[0, 8], [1, 128]],
            channel_multiplier=-1), t_ws)
        VS = SM[:, 42:44]
        VM = SM[:, 44:46]
        t_g = []
        for i in range(2):
            t_g.append(act(VG[:, i, :], ps[i][:, :], ACT.Gelu_apprx_tanh, t_v[i], t_rt, scale=RT[:, i:i + 1],
                           accum_out=VS[:, i:i + 1]))
            bank_free[i] = [t_g[i]]
        t = ts(VM, VS, -1.0 / 512, None, M, None, t_g[1])
        t_xc = [ts(VG[:, i, :], VG[:, i, :], VM[:, i:i + 1], None, ADD, None, t, t_g[i]) for i in range(2)]
        VV = SM[:, 46:48]
        for i in range(2):
            t = act(SM[:, 200:712], VG[:, i, :], ACT.Square, t_xc[i], last("act"), accum_out=VV[:, i:i + 1])
        t = ts(VV, VV, 1.0 / 512, None, M, None, t)
        t = rsqrt(VV, VV, t)
        t_vn = [ts(VG[:, i, :], VG[:, i, :], VV[:, i:i + 1], None, M, None, t) for i in range(2)]

        t_c = []

        def ev_c(j, p, tok):
            t_c.append(tt(CR[:, j, :], p, R2B, M, tok, t_r2b))
            return [t_c[-1]]

        project3(("in1", 2), XGH, XGL, t_xg, ev_c, [0, 1, 2, 7])
        t_cv = []

        def ev_x(j, p, tok):
            z = Z[:, j, 2:258]
            a = tt(z, p, CR[:, j, :], M, tok, t_c[j], t_zpad)
            k = ts(CR[:, j, :], z, vcol("w_conv", 8 + j), None, M, None, a)
            k = stt(CR[:, j, :], Z[:, j, 1:257], vcol("w_conv", 4 + j), CR[:, j, :], M, ADD, k)
            k = stt(CR[:, j, :], Z[:, j, 0:256], vcol("w_conv", j), CR[:, j, :], M, ADD, k)
            t_cv.append(tt(CR[:, j, :], CR[:, j, :], R1B, M, k))
            return [a]

        project3(("in1", 3), XGH, XGL, t_xg, ev_x, [3, 4, 5, 6])
        t_mix, t_sgu = {}, []
        for j in range(4):
            b = 3 + j
            wait("pe", bank_free[b] + [t_msk] + t_vn)
            lst = []
            for hh in range(2):
                h = 2 * j + hh
                for i in range(2):
                    lst.append((ps[b][64 * hh:64 * hh + 64, i * 128:i * 128 + 128], VG[:, i, h * 64:h * 64 + 64],
                                wsv[:, h, :], i == 0, True))
            tok = mms(lst)
            mj = Z[:, j, 2:258]
            mx = mj.rearrange("p (i t) -> p i t", i=2)
            k = None
            for i in range(2):
                k = stt(mx[:, i, :], ps[b][:, i * 128:i * 128 + 128], vcol("g_sgu", j), BB[:, j, :], M, ADD, tok, t_bb,
                        t_cv[j])
            bank_free[b] = [k]
            a = tt(mj, mj, UG[:, j, :], M, k, t_u[j])
            t_sgu.append((mj, act(MIXH[:, 4 + j, :], mj, ACT.Copy, a, t_m)))
        for j in range(4):
            mj, a = t_sgu[j]
            t_mix[4 + j] = tt(MIXL[:, 4 + j, :], mj, MIXH[:, 4 + j, :], SUB, a)
        def ev_b(j, p, tok):
            a = tt(CR[:, j, :], p, CR[:, j, :], M, tok, t_cv[j], t_m)
            t_mix[j] = pair_of(MIXH[:, j, :], MIXL[:, j, :], CR[:, j, :], a)
            return [a]

        project3(("in1", 4), XGH, XGL, t_xg, ev_b, [0, 1, 2, 7])
        t_mixed = all_last()
        for c in range(8):
            t_wrg = ts(wr[:, c, :], wr[:, c, :], vcol("g_ffn", c), None, M, None, t_wr)
        t_x1, t_xT1, t_s2 = {}, {}, []
        R2P = SM[:, 704:708].rearrange("p (n i) -> p n i", n=2)
        R2 = SM[:, 48:50]

        def x1_part(n, i):
            b = [0, 1, 2, 7][2 * n + i]
            tok = wide(b, ("out1", n), MIXH, MIXL, slice(i * 128, i * 128 + 128), t_mix, i == 1,
                       (range(4, 8), range(4)))
            x = XK[:, i, n * 512:n * 512 + 512]
            t_x1[i, n] = tt(x, x, ps[b][:, :], ADD, tok, t_xk)
            bank_free[b] = [t_x1[i, n]]
            return tok

        def x1_turn(n):
            for q in (2 * n, 2 * n + 1):
                b = 3 + q
                tok = tts([(ps[b][:, (cc * 2 + i) * 128:(cc * 2 + i) * 128 + 128],
                            XK[:, i, (2 * q + cc) * 128:(2 * q + cc) * 128 + 128]) for cc in range(2)
                           for i in range(2)], ident, t_x1[0, n], t_x1[1, n], t_cst, *bank_free[b])
                dst = XT[:, 2 * q:2 * q + 2, :].rearrange("p a b -> p (a b)")
                if q % 2:
                    k = act(dst, ps[b][:, :], ACT.Copy, tok)
                else:
                    k = op("dve", lambda e, dst=dst, b=b: e.tensor_copy(dst, ps[b][:, :]), tok)
                bank_free[b] = [k]
                t_xT1[2 * q] = t_xT1[2 * q + 1] = k
            for i in range(2):
                t_s2.append(act(CR[:, 0:2, :].rearrange("p a b -> p (a b)"), XK[:, i, n * 512:n * 512 + 512], ACT.Square,
                                t_x1[i, n], last("act"), scale=1.0 / 32, accum_out=R2P[:, n, i:i + 1]))

        def logits(cs):
            wait("pe", [t_wrg] + bank_free[3] + bank_free[4])
            for c in cs:
                for i in range(2):
                    tok = mms([(ps[3 + i][:, 0:36], XT[:, c, i * 128:i * 128 + 128], wr[:, c, :], c == 0, c == 7)],
                              t_xT1[c])
            return tok

        x1_part(0, 0)
        x1_part(0, 1)
        x1_part(1, 0)
        x1_turn(0)
        t_out1 = x1_part(1, 1)
        logits(range(4))
        x1_turn(1)
        t_lg = logits(range(4, 8))
        t = tt(R2, R2P[:, 0, :], R2P[:, 1, :], ADD, *t_s2)
        t_r2 = rsqrt(R2, R2, t)
        X1H = A(4096, 2, 1024)
        tables("exp_and_others")
        x1h = X1H
        q = [50]

        def small(n):
            v = SM[:, q[0]:q[0] + n]
            q[0] += n
            assert q[0] <= 704
            return v

        LG = small(72).rearrange("p (i n) -> p i n", i=2)
        for i in range(2):
            t = stt(LG[:, i, :], ps[3 + i][:, 0:36], R2[:, i:i + 1], LB, M, ADD, t_lg, t_r2, t_lb)
            bank_free[3 + i] = [t]
        GL = LG[:, :, 0:4]
        EL = LG[:, :, 4:36].rearrange("p i (g e) -> p i g e", g=4)

        def first_max(src, n, t):
            mx = small(2)
            eq = small(2 * n).rearrange("p (i n) -> p i n", i=2)
            mn = small(2)
            t = red(mx, src, ALU.max, t)
            tm = t
            t = tt(eq, src, mx.unsqueeze(2).to_broadcast([128, 2, n]), ALU.is_equal, t)
            t = tt(eq, eq, ix8[:, 0:n].unsqueeze(1).to_broadcast([128, 2, n]), M, t, t_cst)
            t = red(mn, eq, ALU.min, t)
            t = tt(eq, ix8[:, 0:n].unsqueeze(1).to_broadcast([128, 2, n]), mn.unsqueeze(2).to_broadcast([128, 2, n]),
                   ALU.is_equal, t)
            return mx, eq, tm, t

        gm, goh, tm, t_goh = first_max(GL, 4, t)
        ngm = small(2)
        t = ts(ngm, gm, -1.0, None, M, None, tm)
        gex = small(8).rearrange("p (i n) -> p i n", i=2)
        gs = small(2)
        for i in range(2):
            t_gs = act(gex[:, i, :], GL[:, i, :], ACT.Exp, t, bias=ngm[:, i:i + 1], accum_out=gs[:, i:i + 1])
        em = small(64).rearrange("p (i g e) -> p i g e", i=2, g=4)
        t = None
        for i in range(2):
            t = tt(em[:, i], EL[:, i], goh[:, i, :].unsqueeze(2).to_broadcast([128, 4, 8]), M, t_goh)
        es = small(16).rearrange("p (i e) -> p i e", i=2)
        for i in range(2):
            tr = red(es[:, i, :], em[:, i].rearrange("p g e -> p e g"), ALU.add, t)
        v1, oh1, _, t1 = first_max(es, 8, tr)
        e2 = small(16).rearrange("p (i e) -> p i e", i=2)
        t = stt(e2, oh1, -1e30, es, M, ADD, t1)
        v2, oh2, _, t2 = first_max(e2, 8, t)
        dv = small(2)
        t_dv = tt(dv, v2, v1, SUB, t2)
        ex = small(2)
        t_ex = act(ex, dv, ACT.Exp, t_dv)
        t_x1h = [act(X1H[:, i, :], XK[:, i, :], ACT.Copy, t_r2, scale=R2[:, i:i + 1]) for i in range(2)]
        inb = small(16).rearrange("p (i e) -> p i e", i=2)
        mask = small(64).rearrange("p (i g e) -> p i g e", i=2, g=4)
        k = tt(inb, oh1, oh2, ADD, t2)
        for i in range(2):
            gb = goh[:, i, :].unsqueeze(2).to_broadcast([128, 4, 8])
            t_mk = tt(mask[:, i], inb[:, i, :].unsqueeze(1).to_broadcast([128, 4, 8]), gb, M, k)
        mk = mask.rearrange("p i g e -> p i (g e)")
        wait("pe", bank_free[3] + bank_free[4] + [t_mk])
        t_pos = mms([(ps[3][:, 0:32], U, mk[:, 0, :], True, True),
                     (ps[3][:, 32:64], U, mk[:, 1, :], True, False),
                     (ps[3][:, 32:64], one, mk[:, 0, :], False, True),
                     (ps[3][:, 64:96], one, mk[:, 0, :], True, False),
                     (ps[3][:, 64:96], one, mk[:, 1, :], False, True)])
        pos = small(64).rearrange("p (i e) -> p i e", i=2)
        t = stt(pos, ps[3][:, 0:64].rearrange("p (i e) -> p i e", i=2), 1.0, mk, ADD, M, t_pos)
        t_ps = ts(pos, pos, -1.0, None, ADD, None, t)
        cm = small(1)
        t = red(cm, ps[3][:, 64:96], ALU.max, t_pos)
        bank_free[3] = [t]
        t_flag = ts(flag[:], cm, float(CAP), None, ALU.is_gt, None, t)
        comb = small(64).rearrange("p (i g e) -> p i g e", i=2, g=4)
        cb = comb.rearrange("p i g e -> p i (g e)")

        m = o + 2048
        YS = A(2048, 1024)
        SB = [A(m + 256 * k, 2, 2, CAP) for k in range(2)]
        SC = A(m + 512, 2, 2, CAP)
        SCT = [A(x, 256) for x in (m + 768, m + 1024, 3072)]
        SG = A(m + 1280, 512)
        HD = A(m + 1792, 512)
        HT = A(m + 2304, 4, 128)
        HC = [A(6144 + 1024 * k, 8, 2 * CAP) for k in range(2)]
        assert m + 2816 <= o + 4864
        fence = all_last()
        for n in ("dve", "act", "pe"):
            wait(n, fence)
        t_hc, t_sct, t_gat, t_gu, t_scat, t_ys, t_htr, t_dn, t_ht = ({} for _ in range(9))
        t_ctr = {}

        def after(d, k):
            return [d[k]] if k in d else []

        t_pick, t_sc = {}, {}

        def pick(q):
            k = q % 2
            io = iota.unsqueeze(1).to_broadcast([128, 2, CAP])
            for i in range(2):
                pb = pos[:, i, 2 * q:2 * q + 2].unsqueeze(2).to_broadcast([128, 2, CAP])
                t_pick[q] = tt(SB[k][:, i], io, pb, ALU.is_equal, t_ps, *after(t_gat, q - 2))

        def gather(q):
            k = q % 2
            for z in range(2):
                bk = 2 + z
                lst = []
                for c in range(4):
                    for i in range(2):
                        lst.append((ps[bk][:, c * 128:c * 128 + 128],
                                    x1h[:, i, (4 * z + c) * 128:(4 * z + c) * 128 + 128],
                                    SB[k][:, i].rearrange("p e s -> p (e s)"), i == 0, i == 1))
                tok = mms(lst, t_pick[q], *t_x1h, *bank_free[bk])
                g = vec[:, VEC["g_ffn"] + 4 * z:VEC["g_ffn"] + 4 * z + 4].unsqueeze(2).to_broadcast([128, 4, 128])
                t_hc[q] = tt(HC[k][:, 4 * z:4 * z + 4, :], ps[bk][:, :].rearrange("p (c s) -> p c s", c=4), g,
                             M, tok, *after(t_gu, q - 2))
                bank_free[bk] = [t_hc[q]]
            t_gat[q] = tok

        def weigh(q):
            for i in range(2):
                c2 = cb[:, i, 2 * q:2 * q + 2].unsqueeze(2).to_broadcast([128, 2, CAP])
                t_sc[q] = tt(SC[:, i], SB[q % 2][:, i], c2, M, t_pick[q], t_cb, *after(t_ctr, q - 1))

        def turn(q):
            t_ctr[q] = tts([(ps[4][:, i * 128:i * 128 + 128], SC[:, i].rearrange("p e s -> p (e s)"))
                            for i in range(2)], ident, t_sc[q], *bank_free[4])
            t_sct[q] = act(SCT[q % 3], ps[4][:, 0:256], ACT.Copy, t_ctr[q], *after(t_scat, q - 3))
            bank_free[4] = [t_sct[q]]

        def gate_up(q):
            hc = HC[q % 2]
            for bk, key in ((0, "g"), (1, "u")):
                ws = [slot((key, 2 * q + r)) for r in range(2)]
                wv = [w_.rearrange("p (c n) -> p c n", c=8) for w_, _ in ws]
                lst = [(ps[bk][64 * r:64 * r + 64, :], hc[:, c, 64 * r:64 * r + 64], wv[r][:, c, :], c == 0, c == 7)
                       for c in range(8) for r in range(2)]
                tok = mms(lst, ws[0][1], ws[1][1], t_hc[q], *bank_free[bk])
                free((key, 2 * q), tok)
                free((key, 2 * q + 1), tok)
                if key == "g":
                    s = act(SG, ps[0][:, :], ACT.Silu, tok, *after(t_h, q - 1))
                    bank_free[0] = [s]
                    if 1 <= q < NP - 1:
                        turn(q + 1)
            t_gu[q] = tok
            t_h[q] = tt(HD, ps[1][:, :], SG, M, s, tok, *after(t_htr, q - 1))
            bank_free[1] = [t_h[q]]

        t_h = {}

        def down_turn(q):
            t_htr[q] = tts([(ps[4][:, f * 128:f * 128 + 128], HD[:, f * 128:f * 128 + 128]) for f in range(4)], ident,
                           t_h[q], *bank_free[4])
            t_ht[q] = act(HT.rearrange("p a b -> p (a b)"), ps[4][:, :], ACT.Copy, t_htr[q], *after(t_dn, q - 1))
            bank_free[4] = [t_ht[q]]

        def down(q):
            ws = [slot(("d", 2 * q + r)) for r in range(2)]
            wv = [w_.rearrange("p (c n) -> p c n", c=4) for w_, _ in ws]
            t_ys[q] = []
            for n in range(2):
                bk = 5 + n
                lst = [(ps[bk][64 * r:64 * r + 64, :], HT[:, f, 64 * r:64 * r + 64],
                        wv[r][:, f, n * 512:n * 512 + 512], f == 0, f == 3) for f in range(4) for r in range(2)]
                tok = mms(lst, ws[0][1], ws[1][1], t_ht[q], *bank_free[bk])
                k = act(YS[:, n * 512:n * 512 + 512], ps[bk][:, :], ACT.Copy, tok, *after(t_scat, q - 1))
                bank_free[bk] = [k]
                t_ys[q].append(k)
            free(("d", 2 * q), tok)
            free(("d", 2 * q + 1), tok)
            t_dn[q] = tok

        t_acc = {j: t_xT1[2 * j] for j in range(4)}

        def scatter(q):
            for z in range(4):
                bk = [7, 5, 6, 7][z]
                tok = mms([(ps[bk][:, y * 256:y * 256 + 256], YS[:, (2 * z + y) * 128:(2 * z + y) * 128 + 128],
                            SCT[q % 3], True, True) for y in range(2)], t_ys[q][z // 2], t_sct[q], *bank_free[bk])
                x = XT[:, 2 * z:2 * z + 2, :].rearrange("p a b -> p (a b)")
                t_acc[z] = tt(x, x, ps[bk][:, :], ADD, tok, t_acc[z])
                bank_free[bk] = [t_acc[z]]
            t_scat[q] = tok

        pick(0)
        den = small(2)
        t = ts(den, ex, 1.0, None, ADD, None, t_ex)
        t = tt(den, den, gs, M, t, t_gs)
        w1 = small(2)
        t = op("dve", lambda e: e.reciprocal(w1, den), t)
        w2 = small(2)
        t = tt(w2, w1, ex, M, t)
        inn = small(16).rearrange("p (i e) -> p i e", i=2)
        for i in range(2):
            k = ts(inn[:, i, :], oh1[:, i, :], w1[:, i:i + 1], None, M, None, t)
        for i in range(2):
            t = stt(inn[:, i, :], oh2[:, i, :], w2[:, i:i + 1], inn[:, i, :], M, ADD, k)
        for i in range(2):
            gb = goh[:, i, :].unsqueeze(2).to_broadcast([128, 4, 8])
            t_cb = tt(comb[:, i], inn[:, i, :].unsqueeze(1).to_broadcast([128, 4, 8]), gb, M, t)
        gather(0)
        for q in range(NP):
            if q == 2:
                w, t_w = slot(("pproj", 0))
                w = w.rearrange("p (c n) -> p c n", c=4)
                for h in range(4):
                    b = (7, 2, 3, 7)[h]
                    tok = mms([(ps[b][:, y * 256:y * 256 + 256], w[:, c, (2 * h + y) * 128:(2 * h + y) * 128 + 128],
                                PT[:, c, :], c == 0, c == 1) for y in range(2) for c in range(2)],
                              t_w, t_pT, *bank_free[b])
                    k = act(PP[:, 2 * h:2 * h + 2, :].rearrange("p a b -> p (a b)"), ps[b][:, :], ACT.Copy, tok)
                    bank_free[b] = [k]
                    t_pp += [k, k]
                free(("pproj", 0), tok)
            if q + 1 < NP:
                pick(q + 1)
                if q:
                    weigh(q + 1)
            gate_up(q)
            if q == 0:
                for x in range(2):
                    weigh(x)
                    turn(x)
            if q:
                scatter(q - 1)
            down_turn(q)
            if q + 1 < NP:
                gather(q + 1)
            down(q)
        scatter(NP - 1)

        fence = all_last()
        HO = A(10240, 8, 256)
        WG = [A(2048 + 1024 * k, 8, 128) for k in range(2)]
        OH = A(6144, 4, 256)
        WD = A(6144 + 1024, 4, 128)
        OS = A(6144 + 1536, 256)
        CO = A(o, 2, 32)
        COT = A(o + 64, 256)
        s_over = {n: sem("over_" + n) for n in ("pe", "dve", "act", "g", "u", "d")}
        over = {n: [] for n in names}
        ocnt = {n: 0 for n in s_over}

        def oop(eng, fn, *toks):
            for s, v in toks:
                over[eng].append(lambda e, s=s, v=v: e.wait_ge(s, v))
            ocnt[eng] += 1
            over[eng].append(lambda e: fn(e).then_inc(s_over[eng], 1))
            return (s_over[eng], ocnt[eng])

        def oload(which, dst, src, *toks):
            for s, v in toks:
                over["act"].append(lambda e, s=s, v=v: e.wait_ge(s, v))
            ocnt[which] += 16
            over["act"].append(lambda e: e.dma_start(dst, src).then_inc(s_over[which], 16))
            return (s_over[which], ocnt[which])

        def omm(lst, *toks):
            for s, v in toks:
                over["pe"].append(lambda e, s=s, v=v: e.wait_ge(s, v))
            for o_, l, r, a, z in lst[:-1]:
                over["pe"].append(lambda e, o_=o_, l=l, r=r, a=a, z=z: e.matmul(
                    o_, l, r, start=a, stop=z, skip_group_check=True))
            o_, l, r, a, z = lst[-1]
            return oop("pe", lambda e: e.matmul(o_, l, r, start=a, stop=z, skip_group_check=True))

        t = None
        for c in range(8):
            for i in range(2):
                tp = oop("pe", lambda e, c=c, i=i: e.transpose(
                    ps[0][:, i * 128:i * 128 + 128], x1h[:, i, c * 128:c * 128 + 128], ident), *([t] if t else []))
            t = oop("dve", lambda e, c=c: e.tensor_scalar(HO[:, c, :], ps[0][:, 0:256], vcol("g_ffn", c), None, M), tp)
        k = oop("dve", lambda e: e.tensor_scalar(CO, pos, float(CAP) - 0.5, None, ALU.is_ge))
        k = oop("dve", lambda e: e.tensor_tensor(CO, CO, cb, M), k)
        for i in range(2):
            tp = oop("pe", lambda e, i=i: e.transpose(ps[0][0:32, i * 128:i * 128 + 128], CO[:, i, :], ident), k, t)
        t_ready = oop("dve", lambda e: e.tensor_copy(COT[0:32, :], ps[0][0:32, 0:256]), tp)
        t_od = t_ready
        t_wfree = t_dfree = None
        for x in range(NE):
            tb = omm([(ps[1][:, 0:256], ident[0:32, x:x + 1].to_broadcast([32, 128]), COT[0:32, :], True, True)],
                     t_od, t_ready)
            for j in range(4):
                tl = []
                for z, key in enumerate(("g", "u")):
                    src = dr["moe"][moe_at[key, x]].rearrange("p (c n) -> p c n", c=8)[:, :, j * 128:j * 128 + 128]
                    tl.append(oload(key, WG[z], src, *([t_wfree] if t_wfree else [])))
                for z in range(2):
                    tp = omm([(ps[2 + z][:, 0:256], WG[z][:, c, :], HO[:, c, :], c == 0, c == 7) for c in range(8)],
                             tl[z], t_od, tb)
                t_wfree = tp
                ta = oop("act", lambda e: e.activation(OS, ps[2][:, 0:256], ACT.Silu), tp, t_od)
                t_od = oop("dve", lambda e: e.tensor_tensor(OS, OS, ps[3][:, 0:256], M), ta)
                t_od = oop("dve", lambda e, j=j: e.tensor_tensor(OH[:, j, :], OS, ps[1][:, 0:256], M), t_od)
            t_hd = t_od
            for j in range(8):
                src = dr["moe"][moe_at["d", x]].rearrange("p (f n) -> p f n", f=4)[:, :, j * 128:j * 128 + 128]
                tl = oload("d", WD, src, *([t_dfree] if t_dfree else []))
                tp = omm([(ps[4][:, 0:256], WD[:, f, :], OH[:, f, :], f == 0, f == 3) for f in range(4)], tl, t_od)
                t_dfree = tp
                t_od = oop("dve", lambda e, j=j: e.tensor_tensor(XT[:, j, :], XT[:, j, :], ps[4][:, 0:256], ADD), tp)

        def guard(eng):
            wait(eng, fence + [t_flag])

            def emit(e, eng=eng):
                v = e.value_load(flag[0:1, 0:1], min_val=0, max_val=1)
                with e.If(v > 0):
                    for f in over[eng]:
                        f(e)
                    e.wait_ge(*t_od)
            queue[eng].append(emit)

        t_moe = [t_acc[q] for q in range(4)]
        ensure(4 * N0 + 2)
        for eng in ("pe", "dve", "act"):
            guard(eng)

        XN = A(2048, 8, 256)
        XGH, XGL = rounded("ple_h", o + 2560, 8, 256), rounded("ple_l", o + 4608, 8, 256)
        H5H, H5L = rounded("h5_h", 4096, 8, 256), rounded("h5_l", 6144, 8, 256)
        XN2 = A(8192, 8, 256)
        SQ = A(10240, 8, 256)
        RB = A(o + 512, 4, 256)
        TM = A(o + 1536, 4, 256)
        RC, R45 = A(o, 2), A(o + 256, 256)
        t_xg = []
        for c in range(8):
            a = act(XGH[:, c, :], XT[:, c, :], ACT.Copy, t_moe[c // 2], scale=vcol("g_ple", c))
            t_xg.append(stt(XGL[:, c, :], XT[:, c, :], vcol("g_ple", c), XGH[:, c, :], M, SUB, a))
            if c == 4:
                ensure(emitted[0] + 1)
        t_sq = squares(SQ, XT, [t_moe[c // 2] for c in range(8)])
        ensure(4 * N0 + 5)
        t_p = []
        t_gate, t_xn, t_g3, t_sq1, t_sq2, t_h5 = [], [], [], [], [], []

        def ple_gate(j):
            b, tok = t_p[j]
            k = j % 4
            a = tt(TM[:, k, :], ps[b][:, 0:256], RB[:, 0, :], M, tok, t_r3, *([t_xn[j - 4]] if j >= 4 else []))
            bank_free[b] = [a]
            t_gate.append(act(TM[:, k, :], TM[:, k, :], ACT.Sigmoid, a))

        def ple_sum(j):
            k = j % 4
            a = tt(TM[:, k, :], TM[:, k, :], PP[:, j, :], M, t_gate[j], t_pp[j])
            a = tt(XT[:, j, :], XT[:, j, :], TM[:, k, :], ADD, a)
            t_xn.append(a)
            t_g3.append(ts(XN[:, j, :], XT[:, j, :], vcol("g_final", j), None, M, None, a))

        def ple_parts(j):
            g = t_g3[j]
            h = act(H5H[:, j, :], XN[:, j, :], ACT.Copy, g, scale=vcol("pre2", j))
            t_sq1.append(act(SQ[:, j, :], XT[:, j, :], ACT.Square, t_xn[j], t_m))
            t_h5.append(stt(H5L[:, j, :], XN[:, j, :], vcol("pre2", j), H5H[:, j, :], M, SUB, h))
            t_sq2.append(tt(XN2[:, j, :], XN[:, j, :], XN[:, j, :], M, g, eng="pool"))

        def sums(c):
            for b, v, t in ((6, SQ, t_sq1[c]), (7, XN2, t_sq2[c])):
                k = mms([(ps[b][:, 0:256], inv1024, v[:, c, :], c == 0, c == 7)], t, *(bank_free[b] if c == 0 else []))
            return k

        for j in range(8):
            if j == 1:
                t_m = mean_pe(7, 0, SQ, inv1024, t_sq)
                t_r3 = rsqrt(RB[:, 0, :], ps[7][:, 0:256], t_m)
                bank_free[7] = [t_r3]
                tables("sigmoid_and_others")
            b = j % 6
            wait("pe", bank_free[b])
            t_p.append((b, three(ps[b][:, 0:256], ("pgate", j // 4), j % 4, XGH, XGL, t_xg)))
            if j >= 1:
                ple_gate(j - 1)
            ensure(4 * N0 + j + 6)
            if j >= 2:
                ple_sum(j - 2)
            if j >= 3:
                ple_parts(j - 3)
            if j >= 4:
                sums(j - 4)
        ple_gate(7)
        ple_sum(6)
        ple_parts(5)
        ple_sum(7)
        ple_parts(6)
        ple_parts(7)
        ensure(4 * N0 + 14)
        for c in range(4, 7):
            sums(c)

        t_in = []
        for j in range(4):
            wait("pe", bank_free[j])
            t_in.append(three(ps[j][:, 0:256], ("in2", 0), j, H5H, H5L, t_h5))
            if j == 0:
                t_m2 = sums(7)
                t_r4 = rsqrt(RB[:, 1, :], ps[6][:, 0:256], t_m2)
                a = tt(RB[:, 2, :], RB[:, 1, :], RB[:, 1, :], M, t_r4)
                a = tt(RB[:, 2, :], RB[:, 2, :], ps[7][:, 0:256], M, a)
                bank_free[6] = bank_free[7] = [a]
                a = rsqrt(RB[:, 2, :], RB[:, 2, :], a)
                t_r45 = tt(R45, RB[:, 2, :], RB[:, 1, :], M, a)
                tables("sigmoid_and_others")
            ensure(n_piece[("in2", 0), j] + 7)
        t_x4 = [tt(XT[:, c, :], XN[:, c, :], RB[:, 1, :], M, t_r4) for c in range(8)]
        SGC = A(2048, 8, 256)
        SGA = A(o + 512, 8, 256)
        CU = A(10240, 4, 286)
        CA = A(8192, 4, 256)
        QT = A(8192 + 1024, 4, 256)
        KT = A(o + 2560, 4, 256)
        VT = A(o + 3584, 2, 512)
        ZM = A(11384, 2, 384)
        AB = A(o + 4608, 2, 384)
        ATH, ATL = rounded("at_h", o + 5376, 4, 256), rounded("at_l", o + 6400, 4, 256)
        assert 11384 + 768 <= o

        GS = KT
        t_gs = []

        for j in range(4):
            a = tt(GS[:, j, :], ps[j][:, 0:256], R45, M, t_in[j], t_r45)
            bank_free[j] = [a]
            a = act(GS[:, j, :], GS[:, j, :], ACT.Sigmoid, a)
            t_gs.append(tt(GS[:, j, :], GS[:, j, :], R45, M, a))
        tables("natural_log_exp_and_others")
        t_cpad = op("dve", lambda e: e.memset(CU[:, :, 0:30], 0.0))
        t_glu = []

        def ev_glu(j, p, tok):
            t_glu.append(tt(CU[:, j, 30:286], p, GS[:, j, :], M, tok, t_gs[j]))
            return [t_glu[-1]]

        project3(("in2", 1), H5H, H5L, t_h5, ev_glu, [4, 5, 6, 7])
        t_tap, t_add = {}, {}
        TP = A(19712, 4, 256)

        def tap(j, k):
            src = CU[:, j, k:k + 256]
            wv = vec[:, VEC["dw_w"] + 4 * k + j:VEC["dw_w"] + 4 * k + j + 1]
            if k == 0:
                t_tap[j] = ts(CA[:, j, :], src, wv, vcol("dw_b", j), M, ADD, t_glu[j], t_cpad, t_m2)
            elif j == 3:
                n = k % 4
                a = act(TP[:, n, :], src, ACT.Copy, t_glu[j], *([t_add[k - 4]] if k > 4 else []), scale=wv)
                t_tap[j] = t_add[k] = tt(CA[:, j, :], CA[:, j, :], TP[:, n, :], ADD, a, t_tap[j], eng="pool")
            else:
                t_tap[j] = stt(CA[:, j, :], src, wv, CA[:, j, :], M, ADD, t_tap[j])

        taps = [(j, k) for k in range(31) for j in range(3)]
        taps3 = [(3, k) for k in range(31)]

        def some_taps(n, n3=0):
            for left, m in ((taps, n), (taps3, n3)):
                for _ in range(min(m, len(left))):
                    tap(*left.pop(0))

        t_q, t_k, t_vv = [], [], []

        def ev_q(j, p, tok):
            t_q.append(tt(QT[:, j, :], p, R45, M, tok, t_m2))
            some_taps(6)
            return [t_q[-1]]

        def ev_k(j, p, tok):
            t_k.append(tt(KT[:, j, :], p, R45, M, tok, t_glu[3]))
            some_taps(6)
            return [t_k[-1]]

        project3(("in2", 2), H5H, H5L, t_h5, ev_q, [0, 1, 2, 3])
        project3(("in2", 3), H5H, H5L, t_h5, ev_k, [4, 5, 6, 7])
        tok = tts([(ps[2][:, i * 128:i * 128 + 128], R45[:, i * 128:i * 128 + 128]) for i in range(2)], ident,
                  t_r45, *bank_free[2])
        t_rc = op("dve", lambda e: e.tensor_copy(RC, ps[2][:, 0:256].rearrange("p (i n) -> p i n", i=2)[:, :, 0]),
                  tok)
        bank_free[2] = [t_rc]
        ensure(n_piece[("in2", 4), 0] + 8)
        for i in range(2):
            tok = wide(i, ("in2", 4), H5H, H5L, slice(i * 128, i * 128 + 128), t_h5, i == 1)
            t_vv.append(act(VT[:, i, :], ps[i][:, :], ACT.Copy, tok, t_rc, scale=RC[:, i:i + 1]))
            bank_free[i] = [t_vv[i]]
        ensure(n_piece[("in2", 4), 0] + 10)
        some_taps(13)
        t_zm, t_av, t_c2 = {}, {}, {}

        def scores(h):
            b = 2 + h % 2
            r = 64 * (h % 2)
            j = h // 2
            tok = mms([(ps[b][:, 0:256], KT[r:r + 64, j, 0:128], QT[r:r + 64, j, :], True, True),
                       (ps[b][:, 256:384], KT[r:r + 64, j, 128:256], QT[r:r + 64, j, 128:256], True, True)],
                      t_q[j], t_k[j], *bank_free[b])
            k = h % 2
            old = [t_c2[h - 2]] if h >= 2 else []
            t_zm[h] = stt(ZM[:, k, :], ps[b][:, 0:384], 0.125, nm, M, ADD, tok, *old)
            bank_free[b] = [t_zm[h]]
            old = [t_av[h - 2]] if h >= 2 else []
            x = AB[:, k, :]
            a = act(x, ZM[:, k, :], ACT.Abs, t_zm[h], *old)
            a = act(x, x, ACT.Exp, a, scale=-1.0)
            a = act(x, x, ACT.Ln, a, bias=1.0)
            return stt(x, ZM[:, k, :], 0.0, x, MAX, ADD, a)

        def suffix(h, t_p):
            b = 4 + h % 2
            k = h % 2
            x = AB[:, k, :]
            tok = mms([(ps[b][:, 0:256], tri, x[:, 0:256], True, False),
                       (ps[b][:, 128:256], one, x[:, 256:384], False, True),
                       (ps[b][:, 256:384], tri, x[:, 256:384], True, True)], t_p, *bank_free[b])
            a = tt(x, ZM[:, k, :], ps[b][:, 0:384], SUB, tok)
            t_c2[h] = a
            bank_free[b] = [a]
            return act(x, x, ACT.Exp, a)

        t_attT = [None] * 4

        def values(h, t_a):
            b = 6 + (h // 2) % 2
            r = 64 * (h % 2)
            x = AB[:, h % 2, :]
            tok = mms([(ps[b][r:r + 64, 0:256], VT[:, 0, h * 64:h * 64 + 64], x[:, 0:256], True, False),
                       (ps[b][r:r + 64, 128:256], VT[:, 1, h * 64:h * 64 + 64], x[:, 256:384], False, True)],
                      t_a, *t_vv, *(bank_free[b] if h % 2 == 0 else []))
            t_av[h] = tok
            if h % 2:
                j = h // 2
                a = act(ATH[:, j, :], ps[b][:, 0:256], ACT.Copy, tok)
                t_attT[j] = tt(ATL[:, j, :], ps[b][:, 0:256], ATH[:, j, :], SUB, a)
                bank_free[b] = [t_attT[j]]

        t_sg = {}

        def gates(n, j):
            key = ("in2", 5 + n)
            dst = SGC if n < 2 else SGA
            b = j % 2
            wait("pe", bank_free[b])
            tok = three(ps[b][:, 0:256], key, j, H5H, H5L, t_h5)
            jj = 4 * (n % 2) + j
            t_sg[n // 2, jj] = tt(dst[:, jj, :], ps[b][:, 0:256], R45, M, tok, t_x4[7], t_h5[7])
            bank_free[b] = [t_sg[n // 2, jj]]
            ensure(n_piece[key, j] + 7)

        p, a_ = {}, {}
        chunks = [(n, j) for n in range(4) for j in range(4)]
        for s in range(9):
            if s < 8:
                p[s] = scores(s)
            if 1 <= s < 8:
                gates(*chunks.pop(0))
            if s >= 1:
                a_[s - 1] = suffix(s - 1, p[s - 1])
            some_taps(2, 2)
            gates(*chunks.pop(0))
            if s >= 1:
                values(s - 1, a_[s - 1])
            some_taps(2, 2)
        some_taps(1000, 1000)

        fence = all_last() + [last("pool")]
        TMP = A(6144, 4, 256)
        RS = A(6144 + 1280, 256)
        CAH, CAL = rounded("ca_h", 4096, 4, 256), rounded("ca_l", 5120, 4, 256)
        tables("sqrt_and_others")
        wait("act", fence)
        wait("dve", fence)
        t_ma, t_xc, t_s = [], [], []
        t_m = mean_pe(0, 0, CA, inv512, [t_tap[x] for x in range(4)])
        for x in range(4):
            t_xc.append(tt(CA[:, x, :], CA[:, x, :], ps[0][:, 0:256], SUB, t_m))
            t_s.append(act(TMP[:, x, :], CA[:, x, :], ACT.Square, t_xc[x]))
        bank_free[0] = [t_xc[3]]

        def branch(j):
            b = 2 + j % 6
            wait("pe", bank_free[b])
            tok = three(ps[b][:, 0:256], ("ab", 0), j // 2, ATH, ATL, t_attT, cn=4, sub=j % 2, last_use=j % 2)
            return b, tok

        ensure(n_piece[("ab", 0), 0] + 8)
        first = branch(0)
        t_m = mean_pe(1, 0, TMP, inv512, t_s)
        t_rs = rsqrt(RS, ps[1][:, 0:256], t_m)
        bank_free[1] = [t_rs]
        t = [tt(CA[:, x, :], CA[:, x, :], RS, M, t_rs) for x in range(4)]
        for n, v in ((1, SGA), (0, SGC)):
            v = v.rearrange("p a b -> p (a b)")
            t_sg[n] = act(v, v, ACT.Sigmoid, t_sg[n, 7])
        t = [act(CA[:, x, :], CA[:, x, :], ACT.Silu, t[x], scale=vcol("ln_g", x), bias=vcol("ln_b", x))
             for x in range(4)]
        t_hi4 = [act(CAH[:, x, :], CA[:, x, :], ACT.Copy, t[x]) for x in range(4)]
        tables("sqrt_and_others")
        for j in range(8):
            b, tok = branch(j) if j else first
            a = tt(SGA[:, j, :], SGA[:, j, :], ps[b][:, 0:256], M, tok, t_sg[1])
            bank_free[b] = [a]
            t_ma.append(a)
            if j == 5:
                t_cs = [tt(CAL[:, x, :], CA[:, x, :], CAH[:, x, :], SUB, t_hi4[x]) for x in range(4)]
        ensure(n_piece[("ab", 0), 3] + 7)
        MGH, MGL = rounded("mg_h", 8192, 8, 256), rounded("mg_l", 10240, 8, 256)
        t_mg = []
        for j in range(8):
            b = 5 + j % 3
            wait("pe", bank_free[b])
            tok = three(ps[b][:, 0:256], ("cb", 0), j // 2, CAH, CAL, t_cs, cn=4, sub=j % 2, last_use=j % 2)
            a = stt(SGC[:, j, :], ps[b][:, 0:256], vcol("b_cb", j), SGC[:, j, :], ADD, M, tok, t_sg[0])
            bank_free[b] = [a]
            a = tt(SGC[:, j, :], SGC[:, j, :], SGA[:, j, :], ADD, a, t_ma[j])
            t_mg.append(act(MGH[:, j, :], SGC[:, j, :], ACT.Copy, a, *t_cs))
            if j:
                t_mg[j - 1] = tt(MGL[:, j - 1, :], SGC[:, j - 1, :], MGH[:, j - 1, :], SUB, t_mg[j - 1])
            if j % 2:
                ensure(n_piece[("cb", 0), j // 2] + 7)
        t_mg[7] = tt(MGL[:, 7, :], SGC[:, 7, :], MGH[:, 7, :], SUB, t_mg[7])
        MX = A(2048, 8, 256)
        SQ = A(4096, 8, 256)
        t_mx, t_sq = [], []

        def sum_mix(c):
            return mms([(ps[4][:, 0:256], inv1024, SQ[:, c, :], c == 0, c == 7)], t_sq[c], *bank_free[4])

        for n in range(2):
            def ev(j, p, tok, n=n):
                jj = 4 * n + j
                t_sq.append(act(SQ[:, jj, :], p, ACT.Square, tok, *t_mg))
                t_mx.append(act(MX[:, jj, :], p, ACT.Copy, tok, t_vec, scale=vcol("post2", jj)))
                if jj >= 2:
                    sum_mix(jj - 2)
                return [t_mx[-1]]
            project3(("out2", n), MGH, MGL, t_mg, ev, [0, 1, 2, 3])
        sum_mix(6)
        t_m = sum_mix(7)
        R6 = A(6144 + 1280, 256)
        t_r6 = rsqrt(R6, ps[4][:, 0:256], t_m)
        bank_free[4] = [t_r6]
        XGH, XGL = rounded("up_h", 19712, 8, 256), rounded("up_l", 14336, 8, 256)
        t_x5, t_xg, t_sq = [], [], []
        for j in range(9):
            if j < 8:
                eng = "pool" if j % 2 else "dve"
                a = tt(MX[:, j, :], MX[:, j, :], R6, M, t_r6, t_mx[j], eng=eng)
                t_x5.append(tt(XT[:, j, :], XT[:, j, :], MX[:, j, :], ADD, a, eng=eng))
                t_xg.append(act(XGH[:, j, :], XT[:, j, :], ACT.Copy, t_x5[j], scale=vcol("fpre2", j)))
            if j:
                t_xg[j - 1] = stt(XGL[:, j - 1, :], XT[:, j - 1, :], vcol("fpre2", j - 1), XGH[:, j - 1, :], M, SUB,
                                  t_xg[j - 1])
        t_sq = [act(SQ[:, j, :], XT[:, j, :], ACT.Square, t_x5[j], t_m) for j in range(8)]
        FFH = rounded("ff_h", 8192, 22, 256)
        FFL = [rounded("ff_l0", 16384, 13, 256), rounded("ff_l1", 0, 8, 256), rounded("ff_l2", 14080, 1, 256)]

        def ffl(k):
            return FFL[0][:, k, :] if k < 13 else FFL[1][:, k - 13, :] if k < 21 else FFL[2][:, 0, :]

        TG = A(2048, 4, 256)
        GB = A(3072, 1024)
        R7 = A(13824, 256)
        SM2 = A(21760, 8)
        fence = all_last()
        wait("act", fence)
        wait("dve", fence)
        t_gb = load("act", GB, dr["gpost"].partition_broadcast(128), sem("l_gb"))
        fb = [0, 1, 2, 3, 4, 5, 6]
        ix = [0]
        t_ff = []
        t_x5k = []
        for s in range(11):
            for j in range(2):
                jj = 2 * s + j
                bs = []
                for z in range(2):
                    b = fb[ix[0] % 7]
                    ix[0] += 1
                    wait("pe", bank_free[b])
                    bs.append((b, three(ps[b][:, 0:256], ("fup", s), 2 * j + z, XGH, XGL, t_xg)))
                if jj == 0:
                    t_m = mean_pe(7, 0, SQ, inv1024, t_sq)
                    t_r7 = rsqrt(R7, ps[7][:, 0:256], t_m)
                    bank_free[7] = [t_r7]
                (b0, k0), (b1, k1) = bs
                g = TG[:, jj % 2, :]
                u = TG[:, 2 + jj % 2, :]
                old = [t_ff[jj - 2]] if jj >= 2 else []
                a = tt(g, ps[b0][:, 0:256], R7, M, k0, t_r7, *old)
                bank_free[b0] = [a]
                a = act(g, g, ACT.Silu, a)
                bb = tt(u, ps[b1][:, 0:256], R7, M, k1)
                bank_free[b1] = [bb]
                a = tt(u, u, g, M, a, bb)
                t_ff.append(pair_of(FFH[:, jj, :], ffl(jj), u, a, *(t_x5k if jj >= 13 else [])))
                ensure(n_piece[("fup", s), 2 * j + 1] + 7)
            if s == 4:
                X5 = A(4096, 2, 1024)
                for i in range(2):
                    for q in range(2):
                        b = fb[ix[0] % 7]
                        ix[0] += 1
                        tok = tts([(ps[b][:, c * 128:c * 128 + 128], XT[:, 4 * q + c, i * 128:i * 128 + 128])
                                   for c in range(4)], ident, *t_x5, *bank_free[b])
                        k = act(X5[:, i, q * 512:q * 512 + 512], ps[b][:, :], ACT.Copy, tok, t_m)
                        bank_free[b] = [k]
                        t_x5k.append(k)
        s_out = sem("s_out")
        OUT = A(6144, 2, 1024)
        SCR = A(19712, 2, 1024)
        t_lastup = last("pe")
        for n in range(4):
            wait("pe", bank_free[n])
        def down_ff(k, x):
            key = ("fdn", k // 4)
            i = n_piece[key, k % 4]
            ensure(i + 1)
            sl = slice(x * 128, x * 128 + 128)
            for z, w_ in enumerate((WH, WL)):
                lst = []
                for n in range(2):
                    r_ = w_[:, i % 8, n * 512:n * 512 + 512]
                    b = ps[2 * x + n][:, :]
                    lst.append((b, FFH[:, k, sl], r_, k == 0 and z == 0, k == 21 and z == 1))
                    if z == 0:
                        lst.append((b, ffl(k)[:, sl], r_, False, False))
                tok = mms(lst, t_hi[i] if z == 0 else t_lo[i], t_ff[k])
            if x:
                piece_free[i] = tok
                ensure(i + 7)
            return tok

        for k in range(16):
            down_ff(k, 0)
            down_ff(k, 1)
        for k in range(16, 22):
            t_dn0 = down_ff(k, 0)
        for k in range(16, 22):
            tok = down_ff(k, 1)
        tables("sqrt_and_others")
        for i in range(2):
            ss = SM2[:, 2 * i:2 * i + 2]
            t = [act(SCR[:, i, n * 512:n * 512 + 512], ps[2 * i + n][:, :], ACT.Square, (t_dn0, tok)[i], t_lastup,
                     scale=1.0 / 32, accum_out=ss[:, n:n + 1]) for n in range(2)]
            rr = SM2[:, 4 + i:5 + i]
            a = tt(rr, ss[:, 0:1], ss[:, 1:2], ADD, *t)
            a = rsqrt(rr, rr, a)
            for n in range(2):
                sl = slice(n * 512, n * 512 + 512)
                k = stt(OUT[:, i, sl], ps[2 * i + n][:, :], rr, GB[:, sl], M, M, a, t_gb, t_lastup)
                k = tt(OUT[:, i, sl], OUT[:, i, sl], X5[:, i, sl], ADD, k, *t_x5k)
                load("act", out_ap[0, i * 128:i * 128 + 128, sl], OUT[:, i, sl], s_out, k)
        wait("act", [(s_out, 64)])

        src_of = {"in1": "w_in", "out1": "w_out", "pproj": "w_pp", "pgate": "w_pg", "in2": "w_in2", "cb": "w_cb",
                  "ab": "w_ab", "out2": "w_out2", "fup": "w_up2", "fdn": "w_dn2"}
        for i, (name, n) in enumerate(order):
            src = dr["moe"][moe_at[name, n]] if name in ("g", "u", "d") else dr[src_of[name]][n]
            if (name, n) == ("fdn", 5):
                src = src[:, 0:2048]
            k = place[i][0]
            dst = view(k)[:, 0:src.shape[1]]
            before = max((x for x in range(i) if place[x][0] == k), default=None)
            if before is None and 4 <= k < 8:
                wait("sp", [piece_free[4 * N0 - 1 if k in (4, 6) else 4 * N0 - 5]])
            if before is None and k == 9:
                wait("sp", t_mixed)
            if before is not None:
                wait("sp", freed[before])
            if i == 0:
                dst, src = (v.rearrange("p (c n) -> p c n", c=8) for v in (dst, src))
                halves = [(dst[:, :, x:x + 256], src[:, :, x:x + 256], s) for x, s in ((0, ring_sem[k]), (256, s_half))]
                queue["sp"] += [lambda e, d=d, c=c, s=s: e.dma_start(d, c).then_inc(s, 16) for d, c, s in halves]
                continue
            queue["sp"].append(lambda e, dst=dst, src=src, k=k: e.dma_start(dst, src).then_inc(ring_sem[k], 16))
            queue["sp"] += behind.get(i, [])

        block = ctx.enter_context(nc.Block())

        @block.tensor
        def _(e):
            for f in queue["pe"]:
                f(e)

        @block.vector
        def _(e):
            for f in queue["dve"]:
                f(e)

        @block.scalar
        def _(e):
            for f in queue["act"]:
                f(e)

        @block.gpsimd
        def _(e):
            for f in queue["pool"]:
                f(e)

        @block.sync
        def _(e):
            for f in queue["sp"]:
                f(e)


def _cols(a, n):
    k = a.shape[0]
    w = a.shape[1] // n
    return np.ascontiguousarray(a.reshape(k // 128, 128, n, w).transpose(2, 1, 0, 3)).reshape(n, 128, -1)


def _feat(v):
    return v.reshape(-1, 128).T


def _layout(i):
    r = {}
    x = i["x"][0]
    r["x"] = np.ascontiguousarray(x.reshape(2, 128, 1024).transpose(1, 0, 2))
    r["xT"] = np.ascontiguousarray(x.T.reshape(8, 128, 256).transpose(1, 0, 2))
    r["pT"] = np.ascontiguousarray(i["p"][0, 0].T.reshape(2, 128, 256).transpose(1, 0, 2))
    w = i["w_in"][0]
    r["w_in"] = _cols(np.concatenate([w[:, 1536:2048], w[:, 2048:], w[:, 512:1024], w[:, 1024:1536], w[:, :512]], 1), 5)
    r["w_out"] = _cols(i["w_out"][0], 2)
    pp = i["w_ple_proj"][0]
    r["w_pp"] = _cols(pp, 1)
    r["w_pg"] = _cols(i["w_ple_gate"][0], 2)
    g, u, d = (i[k][0].reshape((NE,) + i[k].shape[3:]) for k in ("w_gate", "w_up", "w_down"))
    src = {"g": g, "u": u, "d": d}
    moe = np.empty((96, 128, SLOT), g.dtype)
    for n, (k, e) in enumerate(moe_order()):
        moe[n] = _cols(src[k][e], 1)[0]
    r["moe"] = moe
    w = i["w_in_2"]
    r["w_in2"] = _cols(np.concatenate([w[:, 512:1024], w[:, 0:512], w[:, 1024:]], 1), 9)
    r["w_cb"] = _cols(i["w_conv_branch_2"], 1)
    r["w_ab"] = _cols(i["w_att_branch_2"], 1)
    r["w_out2"] = _cols(i["w_out_2"], 2)
    w = i["w_ffn_up_2"].reshape(1024, 2, 22, 128).transpose(0, 2, 1, 3).reshape(1024, 5632)
    r["w_up2"] = _cols(w, 11)
    dn = i["w_ffn_down_2"]
    dn = np.concatenate([dn, dn[:256]], 0)
    r["w_dn2"] = np.ascontiguousarray(dn.reshape(6, 4, 128, 1024).transpose(0, 2, 1, 3)).reshape(6, 128, SLOT)
    wr = np.concatenate([i["w_group"][0], i["w_router"][0].transpose(1, 0, 2).reshape(1024, 32)], 1)
    r["wr"] = np.ascontiguousarray(wr.reshape(8, 128, 36).transpose(1, 0, 2))
    r["lbias"] = np.concatenate([i["b_group"][0], i["b_router"][0].reshape(-1)])[None]
    r["wsT"] = np.ascontiguousarray(i["w_spatial"][0].transpose(2, 0, 1)).reshape(128, 1024)
    r["b_sp"] = np.ascontiguousarray(i["b_spatial"][0].reshape(4, 2, 128).transpose(1, 0, 2))
    r["gpost"] = i["norm_ffn_post_2"][None]
    v = [_feat(i["g_mix"][0]), i["w_conv"][0].reshape(12, 128).T, _feat(i["g_sgu"][0]), _feat(i["g_ffn"][0]),
         _feat(i["g_ple"][0]), _feat(i["g_final"]), _feat(i["norm_mix_pre_2"]),
         i["conv_dw_w_2"].reshape(124, 128).T, _feat(i["conv_dw_b_2"]), _feat(i["conv_ln_g_2"]),
         _feat(i["conv_ln_b_2"]), _feat(i["b_conv_branch_2"]), _feat(i["norm_mix_post_2"]),
         _feat(i["norm_ffn_pre_2"])]
    r["vec"] = np.ascontiguousarray(np.concatenate(v, 1))
    c = np.zeros((128, N_CST), np.float32)
    k = np.arange(128)
    c[:, C_ID:C_ID + 128] = np.eye(128)
    c[:, C_U:C_U + 128] = k[:, None] < k[None]
    c[:, C_TRI:C_TRI + 128] = k[:, None] >= k[None]
    nmd = np.where(k[:, None] < k[None], 0.0, -1e30)
    c[:, C_NM:C_NM + 128] = nmd
    c[:, C_NM + 256:C_NM + 384] = nmd
    c[:, C_IOTA:C_IOTA + CAP] = np.arange(CAP)
    c[:, C_IX:C_IX + 8] = np.arange(8) - 64.0
    r["cst"] = c
    return r


def kernel(**inputs):
    import concourse.bacc as bacc
    from concourse.bass_utils import run_bass_kernel_spmd

    nc = bacc.Bacc("TRN2", target_bir_lowering=False, num_devices=1, dynamic_dma_scratch_size=128)
    arrays, dr = {}, {}
    for name, a in _layout({k: np.asarray(v) for k, v in inputs.items()}).items():
        a = np.ascontiguousarray(a)
        arrays["in_" + name] = a
        dr[name] = nc.dram_tensor("in_" + name, a.shape, mybir.dt.from_np(a.dtype), kind="ExternalInput").ap()
    out = nc.dram_tensor("out_0", (1, T, D), F32, kind="ExternalOutput").ap()
    build(nc, dr, out)
    r = run_bass_kernel_spmd(nc, [arrays], core_ids=[0])
    return r.results[0]["out_0"]
```
